# Optimizing a Trainium2 kernel written in Bass

```python
import math
import jax, jax.numpy as jnp
from jax import lax
import numpy as np

D_MODEL = 1024
BATCH = 1
SEQ = 128
DEPTH = 2
DEC_BATCH = 1
DEC_SEQ = 1024
PAST_LEN = 256

GRID_W = 64
N_MIXERS = 2
N_A_LAYERS = (DEPTH + 1) // 2
N_B_LAYERS = DEPTH // 2
EPS = 1e-6
CHUNK = 128
A_WIDTH = 2 * D_MODEL
A_GROUPS = 8
A_GROUP_DIM = A_WIDTH // A_GROUPS
N_HEADS = 8
Q_LORA = 512
KV_LORA = 256
NOPE_DIM = 128
ROPE_DIM = 64
V_DIM = 128
ROPE_AXIS_PAIRS = ROPE_DIM // 4
ROPE_BASE = 10000.0
ATTN_SCALE = 1.0 / math.sqrt(NOPE_DIM + ROPE_DIM)
Q_BLOCK = 128
D_FF = ((8 * D_MODEL // 3 + 255) // 256) * 256

kernel_name = "hybrid_gmlp_mla_diffusion_step"

def _rms_norm(x, g):
    xf = x.astype(jnp.float32)
    y = xf * lax.rsqrt(jnp.mean(xf * xf, axis=-1, keepdims=True) + EPS)
    return (y * g.astype(jnp.float32)).astype(x.dtype)

def _modulate(h, shift, scale):
    return h * (1 + scale) + shift

def _axial_rope_tables(n_tokens):
    rows = n_tokens // GRID_W
    row = jnp.repeat(jnp.arange(rows), GRID_W)
    col = jnp.tile(jnp.arange(GRID_W), rows)
    inv = 1.0 / (ROPE_BASE ** (jnp.arange(ROPE_AXIS_PAIRS, dtype=jnp.float32) / ROPE_AXIS_PAIRS))
    ang = jnp.stack([row, col], axis=-1).astype(jnp.float32)[:, :, None] * inv
    ang = jnp.broadcast_to(ang[:, :, None, :], (rows * GRID_W, 2, 2, ROPE_AXIS_PAIRS))
    ang = ang.reshape(rows * GRID_W, ROPE_DIM)
    return jnp.cos(ang), jnp.sin(ang)

def _apply_rope(x, cos, sin):
    xs = x.reshape(x.shape[:-1] + (2, 2, ROPE_AXIS_PAIRS))
    rot = jnp.concatenate([-xs[..., 1:, :], xs[..., :1, :]], axis=-2).reshape(x.shape)
    return (x * cos + rot * sin).astype(x.dtype)

def _chunk_mlp(h, w_in, v_g, w_s, b_s, w_out):
    B, L, _ = h.shape
    z = jax.nn.gelu(h @ w_in, approximate=False)
    u, v = jnp.split(z, 2, axis=-1)
    v = _rms_norm(v, v_g).reshape(B, L // CHUNK, CHUNK, A_GROUPS, A_GROUP_DIM)
    s = jnp.einsum('gpq,bnqgc->bnpgc', w_s, v) + b_s.T[:, :, None]
    return (u * s.reshape(B, L, A_WIDTH)) @ w_out

def _mla_q(h, w_dq, q_g, w_uq):
    B, L, _ = h.shape
    q = (_rms_norm(h @ w_dq, q_g) @ w_uq).reshape(B, L, N_HEADS, NOPE_DIM + ROPE_DIM)
    return q[..., :NOPE_DIM], q[..., NOPE_DIM:]

def _mla_kv(h, w_dkv, kv_g):
    kv = h @ w_dkv
    return _rms_norm(kv[..., :KV_LORA], kv_g), kv[..., KV_LORA:]

def _mla_attend(q_nope, q_rope, ckv, k_rope, w_ukv, w_o):
    B, Lk, _ = ckv.shape
    Lq = q_nope.shape[1]
    kvu = (ckv @ w_ukv).reshape(B, Lk, N_HEADS, NOPE_DIM + V_DIM)
    k_nope, v = kvu[..., :NOPE_DIM], kvu[..., NOPE_DIM:]
    nb = Lq // Q_BLOCK
    qn = q_nope.reshape(B, nb, Q_BLOCK, N_HEADS, NOPE_DIM).swapaxes(0, 1)
    qr = q_rope.reshape(B, nb, Q_BLOCK, N_HEADS, ROPE_DIM).swapaxes(0, 1)

    def block(args):
        qn_b, qr_b = args
        s = (jnp.einsum('bqhd,bkhd->bhqk', qn_b, k_nope)
             + jnp.einsum('bqhr,bkr->bhqk', qr_b, k_rope))
        p = jax.nn.softmax(s.astype(jnp.float32) * ATTN_SCALE, axis=-1).astype(v.dtype)
        return jnp.einsum('bhqk,bkhd->bqhd', p, v)

    o = lax.map(block, (qn, qr))
    o = o.swapaxes(0, 1).reshape(B, Lq, N_HEADS * V_DIM)
    return o @ w_o

def _swiglu(h, w_in, w_out):
    g, u = jnp.split(h @ w_in, 2, axis=-1)
    return (jax.nn.silu(g) * u) @ w_out

def setup_inputs(seed: int = 0) -> dict:
    key = jax.random.key(seed)
    ks = iter(jax.random.split(key, 40))

    def nrm(shape, scale):
        return jax.random.normal(next(ks), shape, jnp.float32) * scale

    D = D_MODEL
    return {
        "x_prompt": nrm((BATCH, SEQ, D), 1.0),
        "x_sample": nrm((DEC_BATCH, DEC_SEQ, D), 1.0),
        "cache_ckv": nrm((DEC_BATCH, N_B_LAYERS, PAST_LEN, KV_LORA), 1.0),
        "cache_krope": nrm((DEC_BATCH, N_B_LAYERS, PAST_LEN, ROPE_DIM), 1.0),
        "c": nrm((DEC_BATCH, D), 1.0),
        "c_ctx": nrm((D,), 1.0),
        "ada_w": nrm((DEPTH, D, 6 * D), 0.5 * D ** -0.5),
        "ada_b": nrm((DEPTH, 6 * D), 0.1),
        "norm1_g": 1.0 + nrm((DEPTH, D), 0.02),
        "norm2_g": 1.0 + nrm((DEPTH, D), 0.02),
        "a_w_in": nrm((N_A_LAYERS, D, 2 * A_WIDTH), D ** -0.5),
        "a_v_g": 1.0 + nrm((N_A_LAYERS, A_WIDTH), 0.02),
        "a_w_s": nrm((N_A_LAYERS, A_GROUPS, CHUNK, CHUNK), CHUNK ** -0.5),
        "a_b_s": 1.0 + nrm((N_A_LAYERS, A_GROUPS, CHUNK), 0.02),
        "a_w_out": nrm((N_A_LAYERS, A_WIDTH, D), A_WIDTH ** -0.5),
        "b_w_dq": nrm((N_B_LAYERS, D, Q_LORA), D ** -0.5),
        "b_q_g": 1.0 + nrm((N_B_LAYERS, Q_LORA), 0.02),
        "b_w_uq": nrm((N_B_LAYERS, Q_LORA, N_HEADS * (NOPE_DIM + ROPE_DIM)), Q_LORA ** -0.5),
        "b_w_dkv": nrm((N_B_LAYERS, D, KV_LORA + ROPE_DIM), D ** -0.5),
        "b_kv_g": 1.0 + nrm((N_B_LAYERS, KV_LORA), 0.02),
        "b_w_ukv": nrm((N_B_LAYERS, KV_LORA, N_HEADS * (NOPE_DIM + V_DIM)), KV_LORA ** -0.5),
        "b_w_o": nrm((N_B_LAYERS, N_HEADS * V_DIM, D), (N_HEADS * V_DIM) ** -0.5),
        "f_w_in": nrm((DEPTH, D, 2 * D_FF), D ** -0.5),
        "f_w_out": nrm((DEPTH, D_FF, D), D_FF ** -0.5),
        "final_g": 1.0 + nrm((D,), 0.02),
    }

def reference(x_prompt, x_sample, cache_ckv, cache_krope, c, c_ctx,
              ada_w, ada_b, norm1_g, norm2_g,
              a_w_in, a_v_g, a_w_s, a_b_s, a_w_out,
              b_w_dq, b_q_g, b_w_uq, b_w_dkv, b_kv_g, b_w_ukv, b_w_o,
              f_w_in, f_w_out, final_g):
    xc = x_prompt
    ctx_ckv, ctx_kr = [], []
    for i in range(DEPTH):
        mod = (jax.nn.silu(c_ctx) @ ada_w[i] + ada_b[i])[None, None, :]
        sh1, sc1, g1, sh2, sc2, g2 = jnp.split(mod, 6, axis=-1)
        h = _modulate(_rms_norm(xc, norm1_g[i]), sh1, sc1)
        j = i // N_MIXERS
        if i % N_MIXERS == 0:
            out = _chunk_mlp(h, a_w_in[j], a_v_g[j], a_w_s[j], a_b_s[j], a_w_out[j])
        else:
            qn, qr = _mla_q(h, b_w_dq[j], b_q_g[j], b_w_uq[j])
            ckv, kr = _mla_kv(h, b_w_dkv[j], b_kv_g[j])
            ctx_ckv.append(ckv)
            ctx_kr.append(kr)
            out = _mla_attend(qn, qr, ckv, kr, b_w_ukv[j], b_w_o[j])
        xc = xc + g1 * out
        h = _modulate(_rms_norm(xc, norm2_g[i]), sh2, sc2)
        xc = xc + g2 * _swiglu(h, f_w_in[i], f_w_out[i])
    y_prompt = _rms_norm(xc, final_g)
    new_ckv = jnp.stack(ctx_ckv, axis=1)
    new_krope = jnp.stack(ctx_kr, axis=1)

    xs = x_sample
    cos, sin = _axial_rope_tables(x_sample.shape[1])
    for i in range(DEPTH):
        mod = (jax.nn.silu(c) @ ada_w[i] + ada_b[i])[:, None, :]
        sh1, sc1, g1, sh2, sc2, g2 = jnp.split(mod, 6, axis=-1)
        h = _modulate(_rms_norm(xs, norm1_g[i]), sh1, sc1)
        j = i // N_MIXERS
        if i % N_MIXERS == 0:
            out = _chunk_mlp(h, a_w_in[j], a_v_g[j], a_w_s[j], a_b_s[j], a_w_out[j])
        else:
            qn, qr = _mla_q(h, b_w_dq[j], b_q_g[j], b_w_uq[j])
            qr = _apply_rope(qr, cos[:, None, :], sin[:, None, :])
            ckv, kr = _mla_kv(h, b_w_dkv[j], b_kv_g[j])
            kr = _apply_rope(kr, cos, sin)
            ckv_all = jnp.concatenate([cache_ckv[:, j].astype(ckv.dtype), ckv], axis=1)
            kr_all = jnp.concatenate([cache_krope[:, j].astype(kr.dtype), kr], axis=1)
            out = _mla_attend(qn, qr, ckv_all, kr_all, b_w_ukv[j], b_w_o[j])
        xs = xs + g1 * out
        h = _modulate(_rms_norm(xs, norm2_g[i]), sh2, sc2)
        xs = xs + g2 * _swiglu(h, f_w_in[i], f_w_out[i])
    y_sample = _rms_norm(xs, final_g)

    return (y_prompt, y_sample, new_ckv, new_krope)


_drawn_inputs = setup_inputs


def setup_inputs(seed=0):
    import zlib

    import numpy as np

    out = dict(_drawn_inputs(seed))
    spreads = {}
    factors = {'cache_ckv': 8.0,
     'cache_krope': 8.0,
     'norm1_g': 2.782,
     'norm2_g': 6.421,
     'a_v_g': 8.0,
     'a_b_s': 8.0,
     'b_q_g': 8.0,
     'b_kv_g': 8.209,
     'final_g': 8.164}
    for name, (base, spread) in spreads.items():
        noise = np.random.default_rng([zlib.crc32(name.encode()), seed]).standard_normal(out[name].shape)
        drawn = base * np.exp(spread * noise) if base else spread * noise
        out[name] = __import__('jax').numpy.asarray(drawn.astype(out[name].dtype))
    for name, factor in factors.items():
        out[name] = (out[name] * factor).astype(out[name].dtype)
    return out
```

```python
import math
from contextlib import ExitStack, contextmanager

import numpy as np

import concourse.bass as bass
from concourse import mybir

F32 = mybir.dt.float32
F32R = mybir.dt.float32r
ACT = mybir.ActivationFunctionType
ALU = mybir.AluOpType
AX_X = mybir.AxisListType.X

P = 128
D = 1024
DT = D // P
CTX, SMP, PAST = 128, 1024, 256
TOK = CTX + SMP
NB = TOK // P
BANKS, CH = 3, TOK // 3
KEYS = TOK + PAST
AW = 2 * D
GT = AW // P
GROUPS = 8
FF = 2816
FT = FF // P
HEADS, NOPE, ROPE, VD = 8, 128, 64, 128
QL, KVL = 512, 256
QT, CT = QL // P, KVL // P
EPS = 1e-6
SCALE = 1.0 / math.sqrt(NOPE + ROPE)
ADA = 6 * DT
SH1, SC1, G1, SH2, SC2, G2 = (n * DT for n in range(6))
ADA_HEAD = 2 * DT
UNIT = 1024
R_COND, R_BIAS = 0, 2 * DT
V_N1, V_N2, V_AV, V_QG, V_KVG, V_FG, V_END = 0, 16, 32, 48, 52, 54, 62
T0_PROBS = 4 + 2 * NB + 3 * GT + 4
SWAP = [(p + 16) % 32 for p in range(32)]


class Count:

    def __init__(self, n=0):
        self.n, self.i, self.per = n, None, 0

    def at(self, off=0):
        v = self.n + off
        if self.i is None:
            return v
        assert v > 0
        return self.i * self.per + v

    def half(self, off=0):
        v = (self.n + off) // 2
        if self.i is None:
            return v
        assert v >= 0 and self.per % 2 == 0
        return self.i * (self.per // 2) + v

    def odd(self, off=0):
        return (self.n + off) % 2

    def past(self, n):
        return self.i is not None or self.n > n

    def step(self, k=1):
        self.n += k


def span(ps, lo, hi):
    if hi - lo <= CH:
        return ps[:, lo // CH, lo % CH:lo % CH + hi - lo]
    return ps[:, lo // CH:hi // CH, 0:CH]


PARTS = [(0, CTX, 0), (CTX, CH, 1), (CH, TOK, 1)]


@contextmanager
def repeat(eng, times, *streams):
    start = [c.n for c, _ in streams]
    with eng.Fori(0, times) as i:
        for c, per in streams:
            c.i, c.per = i, per
        yield i
    for (c, per), n in zip(streams, start):
        assert c.n == n + per, (c.n, n, per)
        c.n, c.i = n + per * times, None


class Kernel:

    def __init__(self, nc, d, stack):
        self.nc, self.d = nc, d
        top = [16640]

        def place(name, shape, dt=F32, offset=None):
            o = (top[0] if offset is None else offset) + 63 & ~63
            size = int(np.prod(shape[1:])) * 4
            if offset is None:
                top[0] = o + size
            assert o + size <= nc.sbuf_usable_end, (name, o + size)
            return nc.alloc_sbuf_tensor_at(name, shape, dt, offset=o)

        def region(start, *items):
            out = []
            for name, shape, dt in items:
                start = start + 63 & ~63
                out.append(place(name, shape, dt, start))
                start += int(np.prod(shape[1:])) * 4
            return out

        self.x = place("x", [P, DT, TOK])
        self.wraw = place("wraw", [P, 2, UNIT])
        self.whi = place("whi", [P, 2, UNIT], F32R)
        self.wlo = place("wlo", [P, 2, UNIT], F32R)
        tmp_at = top[0] + 63 & ~63
        self.tmp = place("tmp", [P, 4, TOK])
        acc_at = top[0] + 63 & ~63
        self.acc = place("acc", [P, TOK])
        self.rstd = place("rstd", [P, TOK])
        self.ident = place("ident", [P, P])
        self.ones = place("ones", [P, P])
        self.mod = place("mod", [P, 2 * ADA, 2])
        self.gain = place("gain", [P, DT, 2])
        self.vecs = place("vecs", [P, V_END])
        self.bias = place("bias", [P, 2 * ADA])
        self.cond = place("cond", [P, DT, 2])
        self.rv = place("rv", [P, NB])
        self.soft = place("soft", [P, 4, 2])
        self.nck = place("nck", [P, KVL + ROPE])
        rest = top[0] + 63 & ~63
        wide = [P, DT, TOK]
        self.xin, self.aldr, self.rowsa, self.rowsb, self.wsraw = region(
            rest, ("xin", [P, NB, D], F32), ("aldr", [P, 4, 2 * UNIT], F32),
            ("rowsa", [P, P], F32), ("rowsb", [P, P], F32), ("wsraw", [P, GROUPS, P], F32))
        self.hhi, self.hlo, self.ghi, self.glo = region(
            rest, ("hhi", wide, F32R), ("hlo", wide, F32R),
            ("ghi", [P, 2, TOK], F32R), ("glo", [P, 2, TOK], F32R))
        mid = rest + 2 * DT * TOK * 4
        self.vst, self.adv = region(mid, ("vst", [P, 2, TOK], F32), ("adv", [P, 2, UNIT], F32))
        late = mid + 4 * TOK * 4
        self.wst, self.bsb, self.vld, = region(
            late, ("wst", [P, GROUPS, P], F32), ("bsb", [P, GROUPS, P], F32), ("vld", [P, 2, TOK], F32))
        self.adu, = region(late + 2 * UNIT * 4 + 2 * TOK * 4, ("adu", [P, 2, UNIT], F32))
        keys = [P, CT, KEYS]
        self.ckh, self.ckl, self.krh, self.krl, self.ckf = region(
            mid, ("ckh", keys, F32R), ("ckl", keys, F32R), ("krh", [P, KEYS], F32R),
            ("krl", [P, KEYS], F32R), ("ckf", [P, CT, TOK], F32))
        after = mid + (2 * CT + 2) * KEYS * 4
        self.qah, self.qal, self.cs = region(
            rest, ("qah", [P, QT, TOK], F32R), ("qal", [P, QT, TOK], F32R), ("cs", [P, 2, TOK], F32))
        self.csk, = region(acc_at, ("csk", [P, 2, TOK], F32))
        self.qnh, self.qnl, self.qrp, self.kth, self.ktl, self.vh, self.vl = region(
            rest, ("qnh", [P, TOK], F32R), ("qnl", [P, TOK], F32R), ("qrp", [P, TOK], F32R),
            ("kth", [P, KEYS], F32R), ("ktl", [P, KEYS], F32R),
            ("vh", [P, KEYS // P, 2, P], F32R), ("vl", [P, KEYS // P, 2, P], F32R))
        o = rest + (3 * TOK + 2 * KEYS + 4 * KEYS) * 4
        self.oh, self.ol = region(o, ("oh", [P, 2, TOK], F32R), ("ol", [P, 2, TOK], F32R))
        assert o + 4 * TOK * 4 <= mid, (o + 4 * TOK * 4, mid)
        self.qld, = region(o + 4 * TOK * 4, ("qld", [P, TOK], F32))
        self.cin, self.kin = region(tmp_at + 3 * TOK * 4, ("cin", [P, 2, KVL], F32), ("kin", [P, 2, P], F32))
        self.pr, = region(after, ("pr", [P, 2, SMP + PAST], F32))
        self.of, = region(o + 5 * TOK * 4, ("of", [P, 2, 2 * P], F32))
        self.pth, self.ptl, self.qlr = region(
            tmp_at, ("pth", [P, 10, 2, P], F32R), ("ptl", [P, 10, 2, P], F32R), ("qlr", [P, TOK], F32))
        self.yst, = region(rest, ("yst", [P, 2, NB, P], F32))

        self.sets = [stack.enter_context(nc.psum_tensor(f"set{n}", [P, BANKS, 512], F32)) for n in range(2)]
        self.tps = [stack.enter_context(nc.psum_tensor(f"turned{n}", [P, 512], F32)) for n in range(2)]

        self.v_dram = nc.dram_tensor("v_scratch", [GT, P, TOK], F32, kind="Internal").ap()
        self.q_dram = nc.dram_tensor("q_scratch", [HEADS, 2, P, TOK], F32, kind="Internal").ap()

        def sem(name):
            return stack.enter_context(nc.semaphore(name))

        self.wload = [sem("unit_loaded_0"), sem("unit_loaded_1")]
        self.hi_done = sem("unit_hi_done")
        self.lo_done = sem("unit_lo_done")
        self.mm_done = sem("job_done")
        self.freed = [sem("set_freed_0"), sem("set_freed_1")]
        self.t_done = sem("turned")
        self.t_free = [sem("turned_freed_0"), sem("turned_freed_1")]
        self.sq_ready = sem("squares_ready")
        self.sq_used = sem("squares_summed")
        self.rs_ready = sem("mean_square_ready")
        self.rt_ready = sem("rstd_ready")
        self.n_ready = sem("scaled_ready")
        self.hf_ready = sem("modulated_ready")
        self.hh_ready = sem("input_hi_ready")
        self.h_ready = sem("input_ready")
        self.af_ready = sem("hidden_ready")
        self.ah_ready = sem("hidden_hi_ready")
        self.a_ready = sem("hidden_parts_ready")
        self.in_loaded = [sem(f"input_loaded_{n}") for n in range(NB)]
        self.rows_loaded = sem("vector_rows_loaded")
        self.ws_loaded = sem("spatial_loaded")
        self.id_loaded = sem("identity_loaded")
        self.ones_set = sem("ones_set")
        self.al_loaded = [sem(f"ada_head_loaded_{n}") for n in range(4)]
        self.al_used = sem("ada_head_used")
        self.al_read = sem("ada_head_read")
        self.ad_loaded = sem("ada_loaded")
        self.spilled = [sem("v_spilled_0"), sem("v_spilled_1")]
        self.v_loaded = [sem("v_loaded_0"), sem("v_loaded_1")]
        self.vs_ready = sem("v_scaled")
        self.rope_loaded = sem("rope_loaded")
        self.cache_loaded = sem("cache_loaded")
        self.ck_ready = sem("keys_ready")
        self.q_spilled = [sem(f"q_spilled_{n}") for n in range(4)]
        self.qf_ready = sem("q_rope_ready")
        self.q_loaded = sem("q_loaded")
        self.qh_ready = sem("q_hi_ready")
        self.q_ready = sem("q_ready")
        self.kh_ready = sem("kv_hi_ready")
        self.nb_ready = sem("max_ready")
        self.e_ready = sem("exp_ready")
        self.p_ready = sem("probs_ready")
        self.pth_ready = sem("probs_turned_hi")
        self.of_ready = sem("head_out_read")
        self.oh_ready = sem("head_out_hi")
        self.o_ready = sem("head_out_ready")
        self.dv_step = sem("vector_step")
        self.ac_step = sem("scalar_step")
        self.y_ready = sem("y_tile_ready")
        self.stored = sem("outputs_stored")
        self.y_stored = [sem("y_stored_0"), sem("y_stored_1")]


class Engine:

    def __init__(self, k, eng):
        self.k, self.eng, self.nc = k, eng, k.nc
        self.J = Count()
        self.U = Count()
        self.T = Count()
        self.Q = Count()
        self.R = Count()
        self.H = Count()
        self.A = Count()
        self.V = Count()
        self.K = Count()
        self.F = Count()
        self.S = Count()
        self.G = Count()
        self.B = Count()
        self.O = Count()
        self.L = Count()
        self.E = Count()
        self.W = Count()


def tiles(w, dims, k):
    return w.rearrange("(k p) n -> p k n", p=P)


class Loads(Engine):
    def unit(self, halves):
        k, s = self.k, self.U.odd()
        if self.U.past(1):
            self.eng.wait_ge(k.lo_done, self.U.at(-1))
        for lo, n, src in halves:
            self.eng.dma_start(k.wraw[:, s, lo:lo + n].rearrange("p (k c) -> p k c", c=src.shape[-1]), src
                               ).then_inc(k.wload[s], 16)
        self.U.step()

    def in_unit(self, w, col):
        v = w.rearrange("(k p) n -> p k n", p=P)
        self.unit([(n * 512, 512, v[:, 4 * n:4 * n + 4, bass.ds(col, P)]) for n in range(2)])

    def out_unit(self, w, row, half):
        self.unit([(n * 512, 512, w[bass.ds(row + n * P, P), half * 512:half * 512 + 512]
                    .rearrange("p (a c) -> p a c", a=1)) for n in range(2)])

    def ada_load(self, dst, layer, first, n, before):
        k = self.k
        self.eng.wait_ge(k.mm_done, before)
        v = k.d["ada_w"][layer].rearrange("(k p) n -> p k n", p=P)
        for u in range(n):
            self.eng.dma_start(dst[:, u, :].rearrange("p (k c) -> p k c", c=P),
                               v[:, :, bass.ds((first + u) * P, P)]).then_inc(k.ad_loaded, 16)

    def program(self):
        k, d, sp, J = self.k, self.k.d, self.eng, self.J
        sp.dma_start(k.ident[:], d["ident"]).then_inc(k.id_loaded, 16)
        sp.dma_start(k.rowsa[0:8, :], d["c_ctx"].rearrange("(a b) -> a b", b=P)).then_inc(k.rows_loaded, 16)
        sp.dma_start(k.rowsa[8:16, :], d["c"][0].rearrange("(a b) -> a b", b=P)).then_inc(k.rows_loaded, 16)
        sp.dma_start(k.rowsa[16:16 + 2 * ADA, :], d["ada_b"].rearrange("l (a b) -> (l a) b", b=P)
                     ).then_inc(k.rows_loaded, 16)
        for lo, name in ((V_N1, "norm1_g"), (V_N2, "norm2_g"), (V_AV, "a_v_g"), (V_QG, "b_q_g"),
                         (V_KVG, "b_kv_g")):
            src = d[name].rearrange("l (a b) -> (l a) b", b=P)
            sp.dma_start(k.rowsb[lo:lo + src.shape[0], :], src).then_inc(k.rows_loaded, 16)
        sp.dma_start(k.rowsb[V_FG:V_END, :], d["final_g"].rearrange("(a b) -> a b", b=P)
                     ).then_inc(k.rows_loaded, 16)
        for b in range(NB):
            src = d["x_prompt"][0] if b == 0 else d["x_sample"][0, (b - 1) * P:b * P, :]
            sp.dma_start(k.xin[:, b, :], src).then_inc(k.in_loaded[b], 16)
            if b == 0:
                sp.dma_start(k.wsraw[:], d["a_w_s"][0].rearrange("g p q -> p g q")).then_inc(k.ws_loaded, 16)
                sp.dma_start(k.bsb[:].rearrange("p g q -> p (g q)"),
                             d["a_b_s"].rearrange("l g q -> l (g q)").partition_broadcast(P)
                             .rearrange("p a n -> p (a n)")).then_inc(k.ws_loaded, 16)
        first = d["ada_w"][0].rearrange("(k p) n -> p k n", p=P)
        for n in range(ADA_HEAD // 2):
            if n >= 4:
                sp.wait_ge(k.al_used, n - 3)
            sp.dma_start(k.aldr[:, n % 4, :].rearrange("p (k c) -> p k c", k=DT),
                         first[:, :, n * 256:n * 256 + 256]).then_inc(k.al_loaded[n % 4], 16)
        w_in = d["a_w_in"][0]
        self.in_unit(w_in, AW)
        self.in_unit(w_in, AW + P)
        J.step()
        with repeat(sp, GT // 2 - 1, (J, 4), (self.U, 2)) as i:
            for h in range(2):
                self.in_unit(w_in, AW + (2 * i + 2 + h) * P)
                self.ada_load(k.adv, 0, ADA_HEAD + 4 * i + 2 * h, 2, J.at())
                J.step(2)
        for h in range(2):
            self.in_unit(w_in, h * P)
            self.ada_load(k.adv, 0, ADA - 4 + 2 * h, 2, J.at())
            J.step(2)
        J.step()
        J.step()
        with repeat(sp, GT // 2 - 1, (J, 16), (self.U, 4)) as i:
            self.mixer_turn(i, False)
        self.mixer_turn(GT // 2 - 1, True)
        self.ffn(0)
        self.attention()
        self.ffn(1)

    def mixer_turn(self, i, last):
        k, d, J = self.k, self.k.d, self.J
        w_in, w_out = d["a_w_in"][0], d["a_w_out"][0]
        if not last:
            self.in_unit(w_in, (2 * i + 2) * P)
        self.out_unit(w_out, 2 * P * i, 0)
        self.ada_load(k.adu, 1, 6 * i, 2, J.at())
        self.out_unit(w_out, 2 * P * i, 1)
        self.ada_load(k.adu, 1, 6 * i + 2, 1, J.at(2))
        if not last:
            self.in_unit(w_in, (2 * i + 3) * P)
        else:
            self.in_unit(d["f_w_in"][0], 0)
        n = 5 - last
        self.ada_load(k.adu, 1, 6 * i + 3, 2, J.at(5))
        self.ada_load(k.adu, 1, 6 * i + 5, 1, J.at(11 - last))
        if last:
            self.in_unit(d["f_w_in"][0], FF)
        J.step(16 - last)

    def ffn_turn(self, layer, i, last):
        w_in, w_out = self.k.d["f_w_in"][layer], self.k.d["f_w_out"][layer]
        self.in_unit(w_in, FF + (2 * i + 1) * P)
        if not last:
            self.in_unit(w_in, (2 * i + 2) * P)
        self.out_unit(w_out, 2 * P * i, 0)
        self.out_unit(w_out, 2 * P * i, 1)
        if not last:
            self.in_unit(w_in, FF + (2 * i + 2) * P)
            self.in_unit(w_in, (2 * i + 3) * P)

    def ffn(self, layer):
        self.J.step()
        self.in_unit(self.k.d["f_w_in"][layer], P)
        with repeat(self.eng, FT // 2 - 1, (self.U, 6)) as i:
            self.ffn_turn(layer, i, False)
        self.ffn_turn(layer, FT // 2 - 1, True)

    def attention(self):
        k, d = self.k, self.k.d
        w_dq, w_uq, w_dkv = d["b_w_dq"][0], d["b_w_uq"][0], d["b_w_dkv"][0]
        v = w_dkv.rearrange("(k p) n -> p k n", p=P)
        self.unit([(n * 256, 256, v[:, 4 * n:4 * n + 4, KVL:KVL + ROPE]) for n in range(2)])
        for m in range(CT):
            self.in_unit(w_dkv, m * P)
        for m in range(QT):
            self.in_unit(w_dq, m * P)
        q = w_uq.rearrange("(k p) (h c) -> p k h c", p=P, c=NOPE + ROPE)
        with repeat(self.eng, HEADS // 2, (self.U, 2)) as i:
            self.unit([(h * 512, 512, q[:, :, 2 * i + h, 0:NOPE]) for h in range(2)])
            self.unit([(h * 256, 256, q[:, :, 2 * i + h, NOPE:]) for h in range(2)])
        kv = d["b_w_ukv"][0].rearrange("(k p) (h c) -> p k h c", p=P, c=NOPE + VD)
        with repeat(self.eng, HEADS // 2, (self.U, 4)) as i:
            for part in range(2):
                self.unit([(n * 256, 256, kv[:, n, bass.ds(2 * i, 2), part * P:part * P + P])
                           for n in range(CT)])
            self.out_unit(d["b_w_o"][0], 2 * P * i, 0)
            self.out_unit(d["b_w_o"][0], 2 * P * i, 1)
        self.in_unit(d["f_w_in"][1], 0)
        self.in_unit(d["f_w_in"][1], FF)


class Products(Engine):
    def open(self):
        k = self.k
        if self.J.past(1):
            self.eng.wait_ge(k.freed[self.J.odd()], self.J.half())
        return k.sets[self.J.odd()]

    def close(self, last):
        last.then_inc(self.k.mm_done, 1)
        self.J.step()

    def unit_ready(self, off=0):
        self.eng.wait_ge(self.k.lo_done, self.U.at(1 + off))

    def parts(self, ps, weights, moving, cols=CH, inputs_ready=None):
        nc, n, last = self.nc, len(weights), None
        for i in range(n):
            if inputs_ready is not None:
                self.eng.wait_ge(self.k.h_ready, inputs_ready + i + 1)
            (wh, wl), (mh, ml) = weights[i], moving[i]
            for p, (w, m) in enumerate(((wh, mh), (wh, ml), (wl, mh))):
                for b in range(BANKS):
                    last = nc.tensor.matmul(ps[:, b, 0:cols], w, m[:, b * cols:(b + 1) * cols],
                                            start=(i == 0 and p == 0), stop=(i == n - 1 and p == 2))
        return last

    def weight(self, slot, at):
        k = self.k
        return k.whi[:, slot, at:at + P], k.wlo[:, slot, at:at + P]

    def in_job(self, first=False):
        k, s = self.k, self.U.odd()
        ps = self.open()
        self.unit_ready()
        self.close(self.parts(ps, [self.weight(s, n * P) for n in range(DT)],
                              [(k.hhi[:, n, :], k.hlo[:, n, :]) for n in range(DT)],
                              inputs_ready=self.H.n if first else None))
        if first:
            self.H.step(DT)
        self.U.step()

    def out_jobs(self, mh, ml, ready, count):
        s = self.U.odd()
        self.unit_ready()
        if ready is not None:
            self.eng.wait_ge(ready, count)
        for n in range(DT // 2):
            ps = self.open()
            self.close(self.parts(ps, [self.weight(s, a * 512 + n * P) for a in range(2)],
                                  [(mh[:, a, :], ml[:, a, :]) for a in range(2)]))
        self.U.step()

    def ada_job(self, src, n):
        k, nc = self.k, self.nc
        ps = self.open()
        self.V.step(n)
        self.eng.wait_ge(k.ad_loaded, self.V.at() * 16)
        for u in range(n):
            for i in range(DT):
                last = nc.tensor.matmul(ps[:, 0, 2 * u:2 * u + 2], src[:, u, i * P:(i + 1) * P],
                                        k.cond[:, i, :], start=(i == 0), stop=(i == DT - 1))
        self.close(last)

    def turn(self, sources, width=P):
        k, nc, b = self.k, self.nc, self.T.odd()
        if self.T.past(1):
            self.eng.wait_ge(k.t_free[b], self.T.half())
        for n, src in enumerate(sources):
            rows = src.shape[0]
            last = nc.tensor.transpose(k.tps[b][0:src.shape[-1], n * width:n * width + rows], src,
                                       k.ident[0:rows, 0:rows])
        last.then_inc(k.t_done, 1)
        self.T.step()

    def statistics(self):
        k, nc = self.k, self.nc
        ps = self.open()
        self.eng.wait_ge(k.sq_used, self.Q.at())
        for b in range(BANKS):
            last = nc.tensor.matmul(ps[:, b, 0:CH], k.ones[:], k.acc[:, b * CH:(b + 1) * CH],
                                    start=True, stop=True)
        self.close(last)

    def program(self):
        k, pe, nc = self.k, self.eng, self.nc
        pe.wait_ge(k.id_loaded, 16)
        pe.wait_ge(k.rows_loaded, 16 * 9)
        self.turn([k.rowsa[0:2 * DT + 2 * ADA, :]])
        self.turn([k.rowsb[0:V_END, :]])
        pe.wait_ge(k.ws_loaded, 32)
        for n in range(2):
            self.turn([k.wsraw[:, 4 * n + g, :] for g in range(4)])
        for b in range(NB):
            pe.wait_ge(k.in_loaded[b], 16)
            for n in range(2):
                self.turn([k.xin[:, b, (4 * n + f) * P:(4 * n + f + 1) * P] for f in range(4)])
        pe.wait_ge(k.t_free[0], 1)
        ps = k.sets[0]
        for n in range(ADA_HEAD // 2):
            pe.wait_ge(k.al_loaded[n % 4], 16 * (n // 4 + 1))
            for u in range(2):
                for i in range(DT):
                    c = 4 * n + 2 * u
                    last = nc.tensor.matmul(ps[:, 0, c:c + 2],
                                            k.aldr[:, n % 4, i * 256 + u * P:i * 256 + (u + 1) * P],
                                            k.cond[:, i, :], start=(i == 0), stop=(i == DT - 1))
            last.then_inc(k.al_used, 1)
        pe.wait_ge(k.al_read, 1)
        pe.wait_ge(k.ones_set, 1)
        self.mixer()
        self.ffn()
        self.attention()
        self.ffn()
        self.Q.step(DT)
        self.statistics()
        for n in range(DT):
            pe.wait_ge(k.y_ready, n + 1)
            for g in range(3):
                self.turn([k.tmp[:, n % 4, (3 * g + b) * P:(3 * g + b + 1) * P] for b in range(3)])

    def mixer(self):
        k, pe, nc, J, T = self.k, self.eng, self.nc, self.J, self.T
        self.Q.step(DT)
        self.statistics()

        def v_tile(m_even, first=False):
            self.in_job(first)
            self.ada_job(k.adv, 2)
            pe.wait_ge(k.freed[J.odd(-2)], J.half(-2) + 1)
            for g in range(3):
                self.turn([k.tmp[:, m_even, (3 * g + b) * P:(3 * g + b + 1) * P] for b in range(3)])

        v_tile(0, first=True)
        v_tile(1)
        with repeat(pe, GT // 2 - 1, (J, 4), (T, 6), (self.U, 2), (self.V, 4)):
            v_tile(0)
            v_tile(1)
        self.Q.step(GT)
        ps = self.open()
        pe.wait_ge(k.sq_used, self.Q.at())
        for b in range(NB):
            last = nc.tensor.matmul(ps[:, 0, b:b + 1], k.acc[:, b * P:(b + 1) * P], k.ones[:, 0:1],
                                    start=True, stop=True)
        self.close(last)
        self.in_job()
        with repeat(pe, GT // 2 - 1, (J, 16), (self.U, 4), (self.V, 6), (self.A, 2)) as i:
            self.mixer_turn(i, False)
        self.mixer_turn(GT // 2 - 1, True)

    def mix(self, i, m):
        k, nc = self.k, self.nc
        ps = self.open()
        self.eng.wait_ge(k.vs_ready, self.A.at(m + 1))
        for b in range(NB):
            last = nc.tensor.matmul(ps[:, b // 3, b % 3 * P:(b % 3 + 1) * P],
                                    k.vld[:, m, b * P:(b + 1) * P], k.wst[:, i, :],
                                    start=True, stop=True)
        self.close(last)

    def mixer_turn(self, i, last):
        k = self.k
        self.mix(i, 0)
        self.ada_job(k.adu, 2)
        self.in_job()
        self.mix(i, 1)
        self.ada_job(k.adu, 1)
        if not last:
            self.in_job()
        self.A.step(2)
        self.out_jobs(k.ghi, k.glo, k.a_ready, self.A.at())
        self.ada_job(k.adu, 2)
        self.out_jobs(k.ghi, k.glo, None, None)
        self.ada_job(k.adu, 1)

    def ffn_turn(self, last):
        k = self.k
        for _ in range(3 if last else 4):
            self.in_job()
        self.A.step(2)
        self.out_jobs(k.ghi, k.glo, k.a_ready, self.A.at())
        self.out_jobs(k.ghi, k.glo, None, None)

    def ffn(self):
        self.Q.step(DT)
        self.statistics()
        self.in_job(first=True)
        with repeat(self.eng, FT // 2 - 1, (self.J, 12), (self.U, 6), (self.A, 2)):
            self.ffn_turn(False)
        self.ffn_turn(True)

    def attention(self):
        k, pe, nc, J = self.k, self.eng, self.nc, self.J
        self.Q.step(DT)
        self.statistics()
        self.in_job(first=True)
        self.in_job()
        self.in_job()
        pe.wait_ge(k.cache_loaded, 48)
        self.turn([k.cin[:, b, m * P:(m + 1) * P] for m in range(CT) for b in range(2)])
        self.turn([k.kin[:, b, :] for b in range(2)])
        pe.wait_ge(k.ck_ready, 1)
        self.turn([k.tmp[0:ROPE, 2, 0:CTX]])
        self.in_job()
        self.Q.step(CT)
        self.statistics()
        pe.wait_ge(k.ck_ready, 3)
        self.turn([k.ckf[:, m, 0:CTX] for m in range(CT)])
        for _ in range(QT - 1):
            self.in_job()
        self.Q.step(QT)
        self.statistics()
        pe.wait_ge(k.h_ready, self.H.n + QT)
        self.H.step(QT)
        with repeat(pe, HEADS // 2, (J, 4), (self.U, 2)):
            for _ in range(2):
                s = self.U.odd()
                self.unit_ready()
                for h in range(2):
                    ps = self.open()
                    self.close(self.parts(ps, [self.weight(s, (4 * h + n) * P) for n in range(QT)],
                                          [(k.qah[:, n, :], k.qal[:, n, :]) for n in range(QT)]))
                self.U.step()
        with repeat(pe, HEADS // 2, (J, 34), (self.U, 4), (self.T, 50), (self.G, 2),
                    (self.B, 18), (self.O, 10)):
            self.head_pair()

    KEY_CH = ((0, 480), (480, 944), (944, KEYS))

    def keys_job(self, h, s):
        k, nc = self.k, self.nc
        ps = self.open()
        for n in range(CT):
            wh, wl = self.weight(s, (2 * n + h) * P)
            for p, (w, m) in enumerate(((wh, k.ckh), (wh, k.ckl), (wl, k.ckh))):
                for b, (lo, hi) in enumerate(self.KEY_CH):
                    last = nc.tensor.matmul(ps[:, b, 0:hi - lo], w, m[:, n, lo:hi],
                                            start=(n == 0 and p == 0), stop=(n == CT - 1 and p == 2))
        self.close(last)

    def values_job(self, blocks, s):
        k, nc = self.k, self.nc
        ps = self.open()
        for i, b in enumerate(blocks):
            for n in range(CT):
                wh, wl = (w[:, s, n * 256:(n + 1) * 256] for w in (k.whi, k.wlo))
                for p, (c, w) in enumerate(((k.ckh, wh), (k.ckh, wl), (k.ckl, wh))):
                    last = nc.tensor.matmul(ps[:, i // 2, i % 2 * 256:(i % 2 + 1) * 256],
                                            c[:, n, b * P:(b + 1) * P], w,
                                            start=(n == 0 and p == 0), stop=(n == CT - 1 and p == 2))
        self.close(last)

    def scores(self, ps, b):
        k, nc, c = self.k, self.nc, slice(b * P, (b + 1) * P)
        chunks = ((0, 0, CTX),) if b == 0 else ((0, CTX, 512), (1, CTX + 512, 512), (2, CTX + 1024, 256))
        passes = ((k.qnh, k.kth), (k.qnh, k.ktl), (k.qnl, k.kth), (k.qrp, k.krh), (k.qrp, k.krl))
        for p, (q, key) in enumerate(passes):
            for bank, lo, n in chunks:
                last = nc.tensor.matmul(ps[:, bank, 0:n], q[:, c], key[:, lo:lo + n],
                                        start=p == 0, stop=p == len(passes) - 1)
        return last

    def weighted(self, ps, h, pair):
        k, nc = self.k, self.nc
        blocks = range(1) if pair is None else range(1, KEYS // P)
        n = P if pair is None else 2 * P
        for i, b in enumerate(blocks):
            for p, (v, pt) in enumerate(((k.vh, k.pth), (k.vh, k.ptl), (k.vl, k.pth))):
                m = pt[:, i, :, :].rearrange("p a c -> p (a c)")[:, 0:n]
                last = nc.tensor.matmul(ps[:, 2, 256:256 + n], v[:, b, h, :], m,
                                        start=(i == 0 and p == 0), stop=(i == len(blocks) - 1 and p == 2))
        return last

    def probs_turned(self):
        self.eng.wait_ge(self.k.t_free[self.T.odd(-1)], self.T.half(-1) + 1)

    def turn_probs(self, s):
        k = self.k
        self.eng.wait_ge(k.p_ready, self.B.at(s + 1))
        n = 1 if s == 8 else 10
        for g in range(0, n, 4):
            self.turn([k.pr[:, s % 2, b * P:(b + 1) * P] for b in range(g, min(g + 4, n))])

    def head_pair(self):
        k, pe, J = self.k, self.eng, self.J
        ku, vu = self.U.odd(), self.U.odd(1)
        self.unit_ready()
        for h in range(2):
            self.keys_job(h, ku)
            if h == 0:
                self.unit_ready(1)
                self.values_job(range(0, 6), vu)
                self.values_job(range(6, 11), vu)
            else:
                self.U.step(2)
            for n in (-1, -2):
                pe.wait_ge(k.freed[J.odd(n)], J.half(n) + 1)
            self.G.step()
            pe.wait_ge(k.q_ready, self.G.at())
            for s in range(-2, 9):
                job = s + 2 < 9
                if job:
                    ps = self.open()
                    last = self.scores(ps, (s + 3) % 9)
                if s >= 2 and s % 2 == 0:
                    if not job:
                        ps = self.open()
                    self.probs_turned()
                    last = self.weighted(ps, h, s // 2 - 1)
                    job = True
                if job:
                    self.close(last)
                if s >= 0:
                    self.turn_probs(s)
            ps = self.open()
            self.probs_turned()
            self.close(self.weighted(ps, h, None))
            self.B.step(9)
            self.O.step(5)
        self.out_jobs(k.oh, k.ol, k.o_ready, self.O.at())
        self.out_jobs(k.oh, k.ol, None, None)


class Activations(Engine):
    def act(self, out, in_, func=ACT.Copy, **kw):
        return self.nc.scalar.activation(out, in_, func, **kw)

    def split(self, double=False, first=False):
        k, s = self.k, self.U.odd()
        self.eng.wait_ge(k.wload[s], self.U.half() * 32 + 32)
        if not first:
            self.eng.wait_ge(k.mm_done, self.J.at())
        if double:
            o = k.whi[:, s, :].rearrange("p (k a c) -> p k a c", a=2, c=ROPE)
            i = k.wraw[:, s, 0:512].rearrange("p (k a c) -> p k a c", a=1, c=ROPE
                                              ).to_broadcast([P, DT, 2, ROPE])
        else:
            o, i = k.whi[:, s, :], k.wraw[:, s, :]
        self.act(o, i).then_inc(k.hi_done, 1)
        self.U.step()

    def squares(self, src):
        k = self.k
        if self.Q.past(1):
            self.eng.wait_ge(k.sq_used, self.Q.at(-1))
        self.act(k.tmp[:, 2 + self.Q.odd(), :], src, ACT.Square).then_inc(k.sq_ready, 1)
        self.Q.step()

    def root(self, out):
        self.eng.wait_ge(self.k.rs_ready, self.R.at(1))
        self.act(out, out, ACT.Sqrt).then_inc(self.k.rt_ready, 1)
        self.R.step()

    def norm(self, shift):
        k, a = self.k, self.eng
        for n in range(DT):
            self.squares(k.x[:, n, :])
        self.J.step()
        self.root(k.rstd[:])
        for n in range(DT):
            src, hf = k.tmp[:, n % 2, :], k.tmp[:, 2 + n % 2, :]
            a.wait_ge(k.n_ready, self.H.n + n + 1)
            if self.H.n + n >= 2:
                a.wait_ge(k.h_ready, self.H.n + n - 1)
            for lo, hi, c in ((0, CTX, 0), (CTX, TOK, 1)):
                self.act(hf[:, lo:hi], src[:, lo:hi], ACT.Identity, scale=k.gain[:, n, c:c + 1],
                         bias=k.mod[:, shift + n, c:c + 1]).then_inc(k.hf_ready, 1)
            a.wait_ge(k.hf_ready, 2 * (self.E.n + n + 1))
            self.act(k.hhi[:, n, :], hf).then_inc(k.hh_ready, 1)
        self.H.step(DT)
        self.E.step(DT)

    def program(self):
        k, a, T = self.k, self.eng, self.T
        a.wait_ge(k.t_done, 1)
        for c in range(2):
            self.act(k.cond[:, :, c], k.tps[0][:, c * DT:(c + 1) * DT], ACT.Silu)
        self.act(k.bias[:], k.tps[0][:, 2 * DT:2 * DT + 2 * ADA]).then_inc(k.t_free[0], 1)
        a.wait_ge(k.t_done, 2)
        self.act(k.vecs[:], k.tps[1][:, 0:V_END]).then_inc(k.t_free[1], 1)
        for n in range(NB):
            a.wait_ge(k.t_done, 4 + 2 * n + 1)
            self.act(k.x[:, 0:4, n * P:(n + 1) * P], k.tps[0][:].rearrange("p (f c) -> p f c", f=4)
                     ).then_inc(k.t_free[0], 1)
        T.step(4 + 2 * NB)
        a.wait_ge(k.t_free[0], 2 + NB)
        a.wait_ge(k.t_free[1], 2 + NB)
        self.split(first=True)
        self.split(first=True)
        a.wait_ge(k.al_read, 1)
        self.mixer()
        self.ffn(0)
        self.attention()
        self.ffn(1)
        self.eng.wait_ge(k.freed[self.J.odd(-1)], self.J.half(-1) + 1)
        self.eng.wait_ge(k.freed[self.J.odd(-2)], self.J.half(-2) + 1)
        for n in range(DT):
            self.squares(k.x[:, n, :])
        self.J.step()
        self.root(k.rstd[:])

    def gelu(self, dst):
        k = self.k
        self.eng.wait_ge(k.mm_done, self.J.at(1))
        ps = k.sets[self.J.odd()]
        self.act(dst.rearrange("p (b c) -> p b c", b=BANKS), ps[:, :, 0:CH], ACT.Gelu
                 ).then_inc(k.freed[self.J.odd()], 1)
        self.J.step()

    def hidden_hi(self, h, ready=None):
        k = self.k
        self.A.step()
        self.act(k.ghi[:, h, :], k.tmp[:, 1, :]).then_inc(k.ah_ready, 1)

    def mixer(self):
        k, a, J = self.k, self.eng, self.J
        self.norm(SH1)
        with repeat(a, GT // 2, (J, 4), (self.U, 2), (self.Q, 2)):
            for h in range(2):
                self.gelu(k.tmp[:, h, :])
                self.eng.wait_ge(k.freed[self.J.odd(-1)], self.J.half(-1) + 1)
                self.squares(k.tmp[:, h, :])
                self.split()
                J.step()
        self.T.step(3 * GT)
        J.step()
        self.root(k.rv[:])
        self.gelu(k.tmp[:, 0, :])
        self.split()
        with repeat(a, GT // 2 - 1, (J, 16), (self.U, 4), (self.A, 2)) as i:
            self.mixer_turn(i, False)
        self.mixer_turn(GT // 2 - 1, True)

    def mixed(self, i, m):
        k = self.k
        self.eng.wait_ge(k.mm_done, self.J.at(1))
        ps = k.sets[self.J.odd()]
        gain = k.vecs[:, V_AV:V_AV + GT].rearrange("p (g m) -> p g m", m=2)
        self.act(k.tmp[:, 2, :].rearrange("p (b c) -> p b c", b=BANKS), ps[:, :, 0:CH], ACT.Copy,
                 scale=gain[:, i, m:m + 1]).then_inc(k.freed[self.J.odd()], 1)
        self.J.step()
        self.eng.wait_ge(k.af_ready, self.A.at(1))
        self.hidden_hi(m)

    def mixer_turn(self, i, last):
        k, J = self.k, self.J
        self.mixed(i, 0)
        J.step()
        self.gelu(k.tmp[:, 0, :])
        self.split()
        self.mixed(i, 1)
        J.step()
        if not last:
            self.gelu(k.tmp[:, 0, :])
            self.split()
        J.step(4)
        self.split()
        J.step(5)
        self.split()
        J.step()

    def gate(self):
        k = self.k
        self.eng.wait_ge(k.mm_done, self.J.at(1))
        ps = k.sets[self.J.odd()]
        self.act(k.tmp[:, 0, :].rearrange("p (b c) -> p b c", b=BANKS), ps[:, :, 0:CH], ACT.Silu
                 ).then_inc(k.freed[self.J.odd()], 1)
        self.J.step()

    def up(self, h):
        k = self.k
        self.J.step()
        self.eng.wait_ge(k.freed[self.J.odd(-1)], self.J.half(-1) + 1)
        self.hidden_hi(h)

    def ffn_turn(self, last, splits=(1, 1, 1, 1, 1, 1), doubled=None):
        k, J = self.k, self.J
        self.up(0)
        self.split()
        self.gate()
        self.split()
        self.up(1)
        self.split()
        if not last:
            self.gate()
            self.split()
        J.step(4)
        if not last or doubled is not None:
            self.split(double=bool(doubled))
        J.step(4)
        if not last or doubled is not None:
            self.split()

    def ffn(self, layer):
        k = self.k
        self.eng.wait_ge(k.freed[self.J.odd(-1)], self.J.half(-1) + 1)
        self.eng.wait_ge(k.freed[self.J.odd(-2)], self.J.half(-2) + 1)
        self.norm(layer * ADA + SH2)
        self.gate()
        self.split()
        with repeat(self.eng, FT // 2 - 1, (self.J, 12), (self.U, 6), (self.A, 2)):
            self.ffn_turn(False)
        self.ffn_turn(True, doubled=True if layer == 0 else None)

    def wide(self, dst, free=True):
        k = self.k
        self.eng.wait_ge(k.mm_done, self.J.at(1))
        ps = k.sets[self.J.odd()]
        r = self.act(dst.rearrange("p (b c) -> p b c", b=BANKS), ps[:, :, 0:CH])
        r.then_inc(k.freed[self.J.odd()], 1)
        self.J.step()

    def attention(self):
        k, a, J, T = self.k, self.eng, self.J, self.T
        self.eng.wait_ge(k.freed[self.J.odd(-1)], self.J.half(-1) + 1)
        self.eng.wait_ge(k.freed[self.J.odd(-2)], self.J.half(-2) + 1)
        self.norm(ADA + SH1)
        a.wait_ge(k.h_ready, self.H.n)
        self.wide(k.tmp[:, 0, :])
        self.split()
        a.wait_ge(k.ck_ready, 1)
        self.act(k.krh[:, 0:TOK], k.tmp[:, 2, :]).then_inc(k.kh_ready, 1)
        for m in range(CT):
            self.wide(k.ckf[:, m, :])
            self.split()
        a.wait_ge(k.t_done, T.at(1))
        self.act(k.ckh[:, :, TOK:], k.tps[T.odd()][:, 0:CT * PAST].rearrange("p (m c) -> p m c", m=CT)
                 ).then_inc(k.kh_ready, 1)
        T.step()
        a.wait_ge(k.t_done, T.at(1))
        self.act(k.krh[:, TOK:], k.tps[T.odd()][:, 0:PAST]).then_inc(k.kh_ready, 1)
        T.step(2)
        self.wide(k.tmp[:, 0, :])
        self.split()
        self.Q.step(CT)
        J.step()
        self.root(k.rstd[:])
        for m in range(CT):
            a.wait_ge(k.ck_ready, 2 + m)
            self.act(k.ckh[:, m, 0:TOK], k.ckf[:, m, :]).then_inc(k.kh_ready, 1)
        T.step()
        for m in range(1, QT):
            self.wide(k.tmp[:, m, :])
            if m < QT - 1:
                self.split()
            else:
                self.split(double=True)
        self.Q.step(QT)
        J.step()
        self.root(k.rstd[:])
        for m in range(QT):
            a.wait_ge(k.n_ready, self.H.n + m + 1)
            self.act(k.qah[:, m, :], k.tmp[:, m, :]).then_inc(k.hh_ready, 1)
        self.H.step(QT)
        a.wait_ge(k.h_ready, self.H.n)
        self.queries(True, False)
        with repeat(a, HEADS // 2 - 2, (J, 4), (self.U, 2), (self.G, 2)):
            self.queries(False, False)
        self.queries(False, True)
        self.G.n = 0
        with repeat(a, HEADS // 2, (J, 34), (self.U, 4), (self.T, 50), (self.G, 2),
                    (self.B, 18), (self.O, 10), (self.F, 6)):
            self.head_pair()

    def queries(self, first, last):
        k = self.k
        for r in range(2):
            for h in range(2):
                if not first:
                    self.eng.wait_ge(k.q_spilled[2 * r + h], self.G.half() * 16)
                self.wide(k.tmp[:, 2 * r + h, :])
            self.split(double=(r == 1 and not last))
        self.G.step(2)

    def kv_hi(self, parts):
        k = self.k
        for dst, src in parts:
            r = self.act(dst, src)
        r.then_inc(k.kh_ready, 1)

    def head_pair(self):
        k, a, J, T = self.k, self.eng, self.J, self.T
        for h in range(2):
            self.eng.wait_ge(k.mm_done, self.J.at(1))
            ps = k.sets[self.J.odd()]
            self.kv_hi([(k.kth[:, 0:480], ps[:, 0, 0:480]),
                        (k.kth[:, 480:].rearrange("p (b c) -> p b c", b=2), ps[:, 1:3, 0:464])])
            J.step()
            if h == 0:
                for lo, n in ((0, 6), (6, 5)):
                    self.eng.wait_ge(k.mm_done, self.J.at(1))
                    ps = k.sets[self.J.odd()]
                    self.kv_hi(v_parts(k.vh, ps, lo, n))
                    J.step()
            else:
                self.split()
                self.split()
            a.wait_ge(k.q_loaded, self.G.at(1) * 32)
            self.act(k.qnh[:], k.qld[:])
            self.act(k.qrp[:], k.qlr[:]).then_inc(k.qh_ready, 1)
            self.G.step()
            for s in range(-2, 9):
                if s >= 0:
                    self.turned(s)
                job = s + 2 < 9
                if job:
                    self.exponentials(s + 2)
                if s >= 2 and s % 2 == 0:
                    if job:
                        self.F.step()
                        a.wait_ge(k.of_ready, self.F.at())
                    else:
                        J.step()
                        self.eng.wait_ge(k.freed[self.J.odd(-1)], self.J.half(-1) + 1)
                    self.out_hi(h, s // 2 - 1)
            J.step()
            self.eng.wait_ge(k.freed[self.J.odd(-1)], self.J.half(-1) + 1)
            self.out_hi(h, None)
            self.B.step(9)
        J.step(4)
        self.split()
        J.step(4)
        self.split()

    def exponentials(self, s):
        k = self.k
        n = CTX if s == 8 else SMP + PAST
        self.eng.wait_ge(k.mm_done, self.J.at(1))
        ps = k.sets[self.J.odd()]
        self.eng.wait_ge(k.nb_ready, self.B.at(s + 1))
        src = ps[:, 0, 0:n] if s == 8 else ps[:].rearrange("p b c -> p (b c)")[:, 0:n]
        self.act(k.pr[:, s % 2, 0:n], src, ACT.Exp, bias=k.soft[:, 0, s % 2:s % 2 + 1], scale=SCALE,
                 accum_out=k.soft[:, 1, s % 2:s % 2 + 1]).then_inc(k.e_ready, 1)
        self.J.step()

    def turned(self, s):
        k, T = self.k, self.T
        if s % 2 == 0 and s >= 2:
            self.eng.wait_ge(k.mm_done, self.J.at(1))
        for g in range(0, 1 if s == 8 else 10, 4):
            n = 1 if s == 8 else min(4, 10 - g)
            self.eng.wait_ge(k.t_done, T.at(1))
            self.act(k.pth[:, g:g + n, (s + 0) % 2, :],
                     k.tps[T.odd()][:, 0:n * P].rearrange("p (b c) -> p b c", b=n)
                     ).then_inc(k.pth_ready, 1)
            T.step()

    def out_hi(self, h, pair):
        k = self.k
        lo, n = (0, P) if pair is None else (P + 2 * P * pair, 2 * P)
        self.act(k.oh[:, h, lo:lo + n], k.of[:, self.O.odd(), 0:n]).then_inc(k.oh_ready, 1)
        self.O.step()


def v_parts(dst, ps, lo, n):
    out = []
    for b in range(0, n, 2):
        m = min(2, n - b)
        out.append((dst[:, lo + b:lo + b + m, :, :].rearrange("p b h c -> p (b h c)"),
                    ps[:, b // 2, 0:m * 256]))
    return out


class Elementwise(Engine):
    def then(self, ins):
        ins.then_inc(self.k.dv_step, 1)
        self.L.step()
        self.eng.wait_ge(self.k.dv_step, self.L.at())

    def free(self, last):
        last.then_inc(self.k.freed[self.J.odd()], 1)
        self.J.step()

    def split(self, double=False):
        k, s = self.k, self.U.odd()
        self.U.step()
        self.eng.wait_ge(k.hi_done, self.U.at())
        if double:
            o, h = (w[:, s, :].rearrange("p (k a c) -> p k a c", a=2, c=ROPE) for w in (k.wlo, k.whi))
            i = k.wraw[:, s, 0:512].rearrange("p (k a c) -> p k a c", a=1, c=ROPE
                                              ).to_broadcast([P, DT, 2, ROPE])
        else:
            o, h, i = k.wlo[:, s, :], k.whi[:, s, :], k.wraw[:, s, :]
        self.nc.vector.tensor_tensor(o, i, h, ALU.subtract).then_inc(k.lo_done, 1)

    def sum_squares(self, first):
        k, v = self.k, self.nc.vector
        sq = k.tmp[:, 2 + self.Q.odd(), :]
        self.S.step()
        self.eng.wait_ge(k.sq_ready, self.S.at())
        r = v.tensor_copy(k.acc[:], sq) if first else v.tensor_tensor(k.acc[:], k.acc[:], sq, ALU.add)
        r.then_inc(k.sq_used, 1)
        self.Q.step()
        self.eng.wait_ge(k.sq_used, self.Q.at())

    def mean(self, out, src, width):
        k = self.k
        s, n = self.J.odd(), self.J.half() + 1
        self.free(self.nc.vector.tensor_scalar(out, src, 1.0 / width, EPS, ALU.mult, ALU.add))
        self.eng.wait_ge(k.freed[s], n)
        self.nc.vector.reciprocal(out, out).then_inc(k.rs_ready, 1)
        self.R.step()
        self.eng.wait_ge(k.rt_ready, self.R.n)

    def mean_rstd(self, width):
        k = self.k
        self.eng.wait_ge(k.mm_done, self.J.at(1))
        ps = k.sets[self.J.odd()]
        self.mean(k.rstd[:].rearrange("p (b c) -> p b c", b=BANKS), ps[:, :, 0:CH], width)

    def norm(self, layer, gains, scale):
        k, dve, v = self.k, self.eng, self.nc.vector
        s = layer * ADA + scale
        g = gains + layer * DT
        v.scalar_tensor_tensor(k.gain[:], k.mod[:, s:s + DT, :], 1.0,
                               k.vecs[:, g:g + DT].unsqueeze(2).to_broadcast([P, DT, 2]),
                               ALU.add, ALU.mult)
        for n in range(DT):
            self.sum_squares(n == 0)
        self.mean_rstd(D)
        for n in range(DT + 1):
            if n < DT:
                if n >= 2:
                    dve.wait_ge(k.hf_ready, 2 * (self.E.n + n - 1))
                v.tensor_tensor(k.tmp[:, n % 2, :], k.x[:, n, :], k.rstd[:], ALU.mult
                                ).then_inc(k.n_ready, 1)
            if n >= 1:
                dve.wait_ge(k.hh_ready, self.H.n + n)
                v.tensor_tensor(k.hlo[:, n - 1, :], k.tmp[:, 2 + (n - 1) % 2, :], k.hhi[:, n - 1, :],
                                ALU.subtract).then_inc(k.h_ready, 1)
        self.H.step(DT)
        self.E.step(DT)

    def program(self):
        k, dve, v, T = self.k, self.eng, self.nc.vector, self.T
        v.memset(k.ones[:], 1.0).then_inc(k.ones_set, 1)
        dve.wait_ge(k.t_free[0], 1)
        for n in range(2):
            dve.wait_ge(k.t_done, 3 + n)
            v.tensor_copy(k.wst[:, 4 * n:4 * n + 4, :],
                          k.tps[n][:].rearrange("p (g c) -> p g c", g=4)).then_inc(k.t_free[n], 1)
        for n in range(NB):
            dve.wait_ge(k.t_done, 4 + 2 * n + 2)
            v.tensor_copy(k.x[:, 4:8, n * P:(n + 1) * P], k.tps[1][:].rearrange("p (f c) -> p f c", f=4)
                          ).then_inc(k.t_free[1], 1)
        T.step(4 + 2 * NB)
        self.split()
        self.split()
        dve.wait_ge(k.al_used, ADA_HEAD // 2)
        v.tensor_tensor(k.mod[:, 0:ADA_HEAD, :],
                        k.sets[0][:, 0, 0:2 * ADA_HEAD].rearrange("p (t c) -> p t c", c=2),
                        k.bias[:, 0:ADA_HEAD].unsqueeze(2).to_broadcast([P, ADA_HEAD, 2]), ALU.add
                        ).then_inc(k.al_read, 1)
        dve.wait_ge(k.al_read, 1)
        self.mixer()
        self.ffn(0)
        self.attention()
        self.ffn(1)
        for n in range(DT):
            self.sum_squares(n == 0)
        self.mean_rstd(D)
        for n in range(DT + 1):
            if n < DT:
                v.scalar_tensor_tensor(k.tmp[:, n % 4, :], k.x[:, n, :], k.vecs[:, V_FG + n:V_FG + n + 1],
                                       k.rstd[:], ALU.mult, ALU.mult).then_inc(k.y_ready, 1)
            if n >= 1:
                m = n - 1
                if m >= 2:
                    dve.wait_ge(k.y_stored[m % 2], 32 * (m // 2))
                for g in range(3):
                    dve.wait_ge(k.t_done, T.n + 1)
                    v.tensor_copy(k.yst[:, m % 2, 3 * g:3 * g + 3, :].rearrange("p b c -> p (b c)"),
                                  k.tps[T.odd()][:, 0:CH]).then_inc(k.t_free[T.odd()], 1)
                    T.step()

    def ada(self, tile, n):
        k = self.k
        self.eng.wait_ge(k.mm_done, self.J.at(1))
        ps = k.sets[self.J.odd()]
        self.free(self.nc.vector.tensor_tensor(
            k.mod[:, bass.ds(tile, n), :], ps[:, 0, 0:2 * n].rearrange("p (t c) -> p t c", c=2),
            k.bias[:, bass.ds(tile, n)].unsqueeze(2).to_broadcast([P, n, 2]), ALU.add))

    def out_tiles(self, gate, half):
        k, v = self.k, self.nc.vector
        for n in range(half * 4, half * 4 + 4):
            self.eng.wait_ge(k.mm_done, self.J.at(1))
            ps = k.sets[self.J.odd()]
            for lo, hi, c in PARTS:
                src = span(ps, lo, hi)
                dst = k.x[:, n, lo:hi]
                if hi - lo > CH:
                    dst = dst.rearrange("p (b c) -> p b c", c=CH)
                last = v.scalar_tensor_tensor(dst, src, k.mod[:, gate + n, c:c + 1], dst,
                                              ALU.mult, ALU.add)
            self.free(last)

    def scale_v(self, m, times):
        k = self.k
        self.eng.wait_ge(k.v_loaded[m], times)
        vt = k.vld[:, m, :].rearrange("p (b c) -> p b c", b=NB)
        self.nc.vector.tensor_tensor(vt, vt, k.rv[:].unsqueeze(2).to_broadcast([P, NB, P]), ALU.mult
                                     ).then_inc(k.vs_ready, 1)

    def hidden_lo(self, h):
        k = self.k
        self.A.step()
        self.eng.wait_ge(k.ah_ready, self.A.at())
        self.nc.vector.tensor_tensor(k.glo[:, h, :], k.tmp[:, 1, :], k.ghi[:, h, :], ALU.subtract
                                     ).then_inc(k.a_ready, 1)

    def mixer(self):
        k, dve, v, J, T = self.k, self.eng, self.nc.vector, self.J, self.T
        self.norm(0, V_N1, SC1)
        self.then(v.memset(k.acc[:], 0.0))
        self.v_turn(0, True)
        with repeat(dve, GT // 2 - 1, (J, 4), (self.U, 2), (self.Q, 2), (self.S, 2), (T, 6)) as i:
            self.v_turn(i + 1, False)
        self.eng.wait_ge(k.mm_done, self.J.at(1))
        ps = k.sets[self.J.odd()]
        self.mean(k.rv[:], ps[:, 0, 0:NB], AW)
        self.scale_v(0, 16)
        J.step()
        self.split()
        with repeat(dve, GT // 2 - 1, (J, 16), (self.U, 4), (self.A, 2), (self.L, 2)) as i:
            self.mixer_turn(i, False)
        self.mixer_turn(GT // 2 - 1, True)

    def v_turn(self, turn, first):
        k, dve, v, J, T = self.k, self.eng, self.nc.vector, self.J, self.T
        for h in range(2):
            self.sum_squares(False)
            J.step()
            self.ada(ADA_HEAD + 4 * turn + 2 * h, 2)
            if not first:
                dve.wait_ge(k.spilled[h], 16 * turn)
            for g in range(3):
                dve.wait_ge(k.t_done, T.at(1))
                v.tensor_copy(k.vst[:, h, g * CH:(g + 1) * CH], k.tps[T.odd()][:, 0:CH]
                              ).then_inc(k.t_free[T.odd()], 1)
                T.step()
            self.split()

    def mixed(self, i, m, last):
        k, v = self.k, self.nc.vector
        self.J.step()
        self.eng.wait_ge(k.freed[self.J.odd(-1)], self.J.half(-1) + 1)
        s = k.tmp[:, 2, :].rearrange("p (b c) -> p b c", b=NB)
        self.then(v.tensor_tensor(s, s, k.bsb[:, i, :].unsqueeze(1).to_broadcast([P, NB, P]), ALU.add))
        v.tensor_tensor(k.tmp[:, 1, :], k.tmp[:, 2, :], k.tmp[:, 0, :], ALU.mult).then_inc(k.af_ready, 1)
        if not last:
            self.scale_v(1 - m, 16 * (i + 1 + m))
        self.hidden_lo(m)

    def mixer_turn(self, i, last):
        k, J = self.k, self.J
        self.mixed(i, 0, False)
        self.ada(ADA + 6 * i, 2)
        J.step()
        self.split()
        self.mixed(i, 1, last)
        self.ada(ADA + 6 * i + 2, 1)
        if not last:
            J.step()
            self.split()
        self.out_tiles(G1, 0)
        self.split()
        self.ada(ADA + 6 * i + 3, 2)
        self.out_tiles(G1, 1)
        self.split()
        self.ada(ADA + 6 * i + 5, 1)

    def up(self, h):
        k = self.k
        self.eng.wait_ge(k.mm_done, self.J.at(1))
        ps = k.sets[self.J.odd()]
        self.eng.wait_ge(k.freed[self.J.odd(-1)], self.J.half(-1) + 1)
        self.free(self.nc.vector.tensor_tensor(
            k.tmp[:, 1, :].rearrange("p (b c) -> p b c", b=BANKS), ps[:, :, 0:CH],
            k.tmp[:, 0, :].rearrange("p (b c) -> p b c", b=BANKS), ALU.mult))
        self.hidden_lo(h)

    def ffn_turn(self, gate, last, doubled=None):
        J = self.J
        self.up(0)
        self.split()
        J.step()
        self.split()
        self.up(1)
        self.split()
        if not last:
            J.step()
            self.split()
        self.out_tiles(gate, 0)
        if not last or doubled is not None:
            self.split(double=bool(doubled))
        self.out_tiles(gate, 1)
        if not last or doubled is not None:
            self.split()

    def ffn(self, layer):
        self.norm(layer, V_N2, SC2)
        self.J.step()
        self.split()
        gate = layer * ADA + G2
        with repeat(self.eng, FT // 2 - 1, (self.J, 12), (self.U, 6), (self.A, 2)):
            self.ffn_turn(gate, False)
        self.ffn_turn(gate, True, doubled=True if layer == 0 else None)

    def rotate(self, out, t, by_cos, partner, cos, sin):
        v = self.nc.vector
        v.tensor_tensor(by_cos, t, cos, ALU.mult)
        self.then(v.stream_shuffle(partner, t, SWAP))
        self.then(v.tensor_tensor(partner, partner, sin, ALU.mult))
        return v.tensor_tensor(out, by_cos, partner, ALU.add)

    def square_into_acc(self, src, first):
        k, v = self.k, self.nc.vector
        if first:
            v.tensor_tensor(k.acc[:], src, src, ALU.mult).then_inc(k.sq_used, 1)
        else:
            self.then(v.tensor_tensor(k.rstd[:], src, src, ALU.mult))
            v.tensor_tensor(k.acc[:], k.acc[:], k.rstd[:], ALU.add).then_inc(k.sq_used, 1)
        self.Q.step()
        self.eng.wait_ge(k.sq_used, self.Q.at())

    def attention(self):
        k, dve, v, J, T = self.k, self.eng, self.nc.vector, self.J, self.T
        self.norm(1, V_N1, SC1)
        J.step()
        self.eng.wait_ge(k.freed[self.J.odd(-1)], self.J.half(-1) + 1)
        dve.wait_ge(k.rope_loaded, 16)
        self.split()
        t0, t2 = k.tmp[:, 0, :], k.tmp[:, 2, :]
        self.rotate(t2, t0, t2, k.tmp[:, 1, :], k.csk[:, 0, :], k.csk[:, 1, :]).then_inc(k.ck_ready, 1)
        dve.wait_ge(k.ck_ready, 1)
        dve.wait_ge(k.kh_ready, 1)
        v.tensor_tensor(k.krl[:, 0:TOK], t2, k.krh[:, 0:TOK], ALU.subtract)
        for m in range(CT):
            J.step()
            self.split()
            self.eng.wait_ge(k.freed[self.J.odd(-1)], self.J.half(-1) + 1)
            self.square_into_acc(k.ckf[:, m, :], m == 0)
        dve.wait_ge(k.kh_ready, 2)
        v.tensor_tensor(k.ckl[:, :, TOK:], k.tps[T.odd()][:, 0:CT * PAST].rearrange("p (m c) -> p m c", m=CT),
                        k.ckh[:, :, TOK:], ALU.subtract).then_inc(k.t_free[T.odd()], 1)
        T.step()
        dve.wait_ge(k.kh_ready, 3)
        v.tensor_tensor(k.krl[:, TOK:], k.tps[T.odd()][:, 0:PAST], k.krh[:, TOK:], ALU.subtract
                        ).then_inc(k.t_free[T.odd()], 1)
        T.step()
        dve.wait_ge(k.t_done, T.at(1))
        v.tensor_copy(k.nck[:, KVL:], k.tps[T.odd()][:, 0:ROPE]).then_inc(k.t_free[T.odd()], 1)
        T.step()
        J.step()
        self.split()
        self.mean_rstd(KVL)
        for m in range(CT):
            v.scalar_tensor_tensor(k.ckf[:, m, :], k.ckf[:, m, :], k.vecs[:, V_KVG + m:V_KVG + m + 1],
                                   k.rstd[:], ALU.mult, ALU.mult).then_inc(k.ck_ready, 1)
        for m in range(CT):
            dve.wait_ge(k.kh_ready, 4 + m)
            v.tensor_tensor(k.ckl[:, m, 0:TOK], k.ckf[:, m, :], k.ckh[:, m, 0:TOK], ALU.subtract)
        dve.wait_ge(k.t_done, T.at(1))
        v.tensor_copy(k.nck[:, 0:KVL], k.tps[T.odd()][:, 0:KVL]).then_inc(k.t_free[T.odd()], 1)
        T.step()
        self.square_into_acc(k.tmp[:, 0, :], True)
        for m in range(1, QT):
            J.step()
            self.eng.wait_ge(k.freed[self.J.odd(-1)], self.J.half(-1) + 1)
            self.square_into_acc(k.tmp[:, m, :], False)
            self.split(double=m == QT - 1)
        self.mean_rstd(QL)
        for m in range(QT):
            v.scalar_tensor_tensor(k.tmp[:, m, :], k.tmp[:, m, :], k.vecs[:, V_QG + m:V_QG + m + 1],
                                   k.rstd[:], ALU.mult, ALU.mult).then_inc(k.n_ready, 1)
        for m in range(QT):
            dve.wait_ge(k.hh_ready, self.H.n + m + 1)
            v.tensor_tensor(k.qal[:, m, :], k.tmp[:, m, :], k.qah[:, m, :], ALU.subtract
                            ).then_inc(k.h_ready, 1)
        self.H.step(QT)
        dve.wait_ge(k.rope_loaded, 32)
        self.queries(True, False)
        with repeat(dve, HEADS // 2 - 2, (J, 4), (self.U, 2), (self.L, 4), (self.W, 2)):
            self.queries(False, False)
        self.queries(False, True)
        with repeat(dve, HEADS // 2, (J, 34), (self.U, 4), (T, 50), (self.G, 2), (self.B, 18),
                    (self.O, 10), (self.F, 6), (self.L, 18), (self.K, 4)):
            self.head_pair()

    def queries(self, first, last):
        k, J = self.k, self.J
        J.step(2)
        self.split()
        for h in range(2):
            J.step()
            self.eng.wait_ge(k.freed[self.J.odd(-1)], self.J.half(-1) + 1)
            if not first or h:
                self.eng.wait_ge(k.qf_ready, self.W.at())
            self.W.step()
            t = k.tmp[:, 2 + h, :]
            self.rotate(t, t, k.rstd[:], k.acc[:], k.cs[:, 0, :], k.cs[:, 1, :]).then_inc(k.qf_ready, 1)
        self.split(double=not last)

    def kv_lo(self, parts):
        k = self.k
        self.K.step()
        self.eng.wait_ge(k.kh_ready, self.K.at(5))
        for dst, hi, src in parts:
            last = self.nc.vector.tensor_tensor(dst, src, hi, ALU.subtract)
        self.free(last)

    def head_pair(self):
        k, dve, v, J = self.k, self.eng, self.nc.vector, self.J
        for h in range(2):
            self.eng.wait_ge(k.mm_done, self.J.at(1))
            ps = k.sets[self.J.odd()]
            self.kv_lo([(k.ktl[:, 0:480], k.kth[:, 0:480], ps[:, 0, 0:480]),
                        (k.ktl[:, 480:].rearrange("p (b c) -> p b c", b=2),
                         k.kth[:, 480:].rearrange("p (b c) -> p b c", b=2), ps[:, 1:3, 0:464])])
            if h == 0:
                for lo, n in ((0, 6), (6, 5)):
                    self.eng.wait_ge(k.mm_done, self.J.at(1))
                    ps = k.sets[self.J.odd()]
                    self.kv_lo([(a, b, c) for (a, c), (b, _) in
                                zip(v_parts(k.vl, ps, lo, n), v_parts(k.vh, ps, lo, n))])
            else:
                self.split()
                self.split()
            self.G.step()
            dve.wait_ge(k.qh_ready, self.G.at())
            v.tensor_tensor(k.qnl[:], k.qld[:], k.qnh[:], ALU.subtract)
            v.tensor_tensor(k.qrp[ROPE:P, :], k.qlr[ROPE:P, :], k.qrp[ROPE:P, :], ALU.subtract
                            ).then_inc(k.q_ready, 1)
            for s in range(-2, 9):
                if s >= 0:
                    self.turned(s)
                job, out = s + 2 < 9, s >= 2 and s % 2 == 0
                if job:
                    self.maxima(s + 2, out)
                elif out:
                    self.eng.wait_ge(k.mm_done, self.J.at(1))
                    ps = k.sets[self.J.odd()]
                    self.free(v.tensor_copy(k.of[:, self.O.odd(), :], ps[:, 2, 256:512]))
                if out:
                    self.out_lo(h, s // 2 - 1)
                if job:
                    self.normalise(s + 2)
            self.eng.wait_ge(k.mm_done, self.J.at(1))
            ps = k.sets[self.J.odd()]
            self.free(v.tensor_copy(k.of[:, self.O.odd(), 0:P], ps[:, 2, 256:256 + P]))
            self.out_lo(h, None)
            self.B.step(9)
        self.out_tiles(ADA + G1, 0)
        self.split()
        self.out_tiles(ADA + G1, 1)
        self.split()

    def maxima(self, s, out):
        k, v = self.k, self.nc.vector
        n = CTX if s == 8 else SMP + PAST
        self.eng.wait_ge(k.mm_done, self.J.at(1))
        ps = k.sets[self.J.odd()]
        src = ps[:, 0, 0:n] if s == 8 else ps[:].rearrange("p b c -> p (b c)")[:, 0:n]
        nmax = k.soft[:, 3, s % 2:s % 2 + 1]
        if out:
            v.tensor_copy(k.of[:, self.O.odd(), :], ps[:, 2, 256:512]).then_inc(k.of_ready, 1)
            self.F.step()
        self.then(v.reduce_max(nmax, src, AX_X, negate=True))
        v.tensor_scalar(k.soft[:, 0, s % 2:s % 2 + 1], nmax, SCALE, None, ALU.mult).then_inc(k.nb_ready, 1)
        self.J.step()

    def normalise(self, s):
        k, v = self.k, self.nc.vector
        n = CTX if s == 8 else SMP + PAST
        inv = k.soft[:, 2, s % 2:s % 2 + 1]
        self.eng.wait_ge(k.e_ready, self.B.at(s + 1))
        v.reciprocal(inv, k.soft[:, 1, s % 2:s % 2 + 1]).then_inc(k.freed[self.J.odd(-1)], 1)
        self.eng.wait_ge(k.freed[self.J.odd(-1)], self.J.half(-1) + 1)
        v.tensor_scalar(k.pr[:, s % 2, 0:n], k.pr[:, s % 2, 0:n], inv, None, ALU.mult
                        ).then_inc(k.p_ready, 1)

    def turned(self, s):
        k, T = self.k, self.T
        for g in range(0, 1 if s == 8 else 10, 4):
            n = 1 if s == 8 else min(4, 10 - g)
            self.eng.wait_ge(k.pth_ready, T.at(1 - T0_PROBS))
            self.nc.vector.tensor_tensor(k.ptl[:, g:g + n, s % 2, :],
                                         k.tps[T.odd()][:, 0:n * P].rearrange("p (b c) -> p b c", b=n),
                                         k.pth[:, g:g + n, s % 2, :], ALU.subtract
                                         ).then_inc(k.t_free[T.odd()], 1)
            T.step()

    def out_lo(self, h, pair):
        k = self.k
        lo, n = (0, P) if pair is None else (P + 2 * P * pair, 2 * P)
        o = self.O.odd()
        self.O.step()
        self.eng.wait_ge(k.oh_ready, self.O.at())
        self.nc.vector.tensor_tensor(k.ol[:, h, lo:lo + n], k.of[:, o, 0:n], k.oh[:, h, lo:lo + n],
                                     ALU.subtract).then_inc(k.o_ready, 1)


class Moves(Engine):
    def program(self):
        k, g, J, T, d = self.k, self.eng, self.J, self.T, self.k.d
        T.step(4 + 2 * NB)
        J.step()
        with repeat(g, GT // 2, (J, 4), (T, 6)) as i:
            for h in range(2):
                T.step(3)
                g.wait_ge(k.t_free[T.odd(-1)], T.half(-1) + 1)
                g.wait_ge(k.t_free[T.odd(-2)], T.half(-2) + 1)
                g.dma_start(k.v_dram[2 * i + h], k.vst[:, h, :]).then_inc(k.spilled[h], 16)
                J.step(2)
        J.step(2)
        for h in range(2):
            g.wait_ge(k.spilled[h], 16 * (GT // 2))
        for h in range(2):
            g.dma_start(k.vld[:, h, :], k.v_dram[h]).then_inc(k.v_loaded[h], 16)
        with repeat(g, GT // 2 - 1, (J, 16)) as i:
            for h in range(2):
                g.wait_ge(k.mm_done, J.at(1 + 3 * h))
                g.dma_start(k.vld[:, h, :], k.v_dram[2 * i + 2 + h]).then_inc(k.v_loaded[h], 16)
            J.step(16)
        J.step(15)
        J.step(2 + 12 * (FT // 2 - 1) + 11 + 1)
        g.wait_ge(k.h_ready, 3 * DT)
        g.dma_start(k.csk[:], d["rope"].rearrange("a p n -> p a n")).then_inc(k.rope_loaded, 16)
        g.dma_start(k.cin[:], d["cache_ckv"][0, 0].rearrange("(b p) n -> p b n", p=P)
                    ).then_inc(k.cache_loaded, 16)
        for c in range(2):
            g.dma_start(k.kin[:, :, c * ROPE:(c + 1) * ROPE],
                        d["cache_krope"][0, 0].rearrange("(b p) n -> p b n", p=P)
                        ).then_inc(k.cache_loaded, 16)
        g.wait_ge(k.t_free[T.odd(2)], T.half(2) + 1)
        g.dma_start(d["new_krope"][0, 0], k.nck[:, KVL:]).then_inc(k.stored, 16)
        g.wait_ge(k.t_free[T.odd(3)], T.half(3) + 1)
        g.dma_start(d["new_ckv"][0, 0], k.nck[:, 0:KVL]).then_inc(k.stored, 16)
        T.step(4)
        J.step(1 + CT + 1 + 1 + QT - 1 + 1)
        g.wait_ge(k.mm_done, J.at())
        g.dma_start(k.cs[:], d["rope"].rearrange("a p n -> p a n")).then_inc(k.rope_loaded, 16)
        with repeat(g, HEADS // 2, (J, 4), (self.G, 2)) as i:
            for h in range(2):
                J.step()
                self.eng.wait_ge(k.freed[self.J.odd(-1)], self.J.half(-1) + 1)
                g.dma_start(k.q_dram[2 * i + h, 0], k.tmp[:, h, :]).then_inc(k.q_spilled[h], 16)
            for h in range(2):
                J.step()
                self.G.step()
                g.wait_ge(k.qf_ready, self.G.at())
                g.dma_start(k.q_dram[2 * i + h, 1], k.tmp[:, 2 + h, :]).then_inc(k.q_spilled[2 + h], 16)
        self.G.n = 0
        for n in range(4):
            g.wait_ge(k.q_spilled[n], 16 * (HEADS // 2))
        g.dma_start(k.qld[:], k.q_dram[0, 0]).then_inc(k.q_loaded, 16)
        g.dma_start(k.qlr[:], k.q_dram[0, 1]).then_inc(k.q_loaded, 16)
        with repeat(g, HEADS - 1) as i:
            g.wait_ge(k.q_ready, i + 1)
            g.dma_start(k.qld[:], k.q_dram[i + 1, 0]).then_inc(k.q_loaded, 16)
            g.dma_start(k.qlr[:], k.q_dram[i + 1, 1]).then_inc(k.q_loaded, 16)
        J.step(34 * (HEADS // 2) + 2 + 12 * (FT // 2 - 1) + 11 + 1)
        T.step(50 * (HEADS // 2))
        for n in range(DT):
            T.step(3)
            g.wait_ge(k.t_free[T.odd(-1)], T.half(-1) + 1)
            g.wait_ge(k.t_free[T.odd(-2)], T.half(-2) + 1)
            c = slice(n * P, (n + 1) * P)
            g.dma_start(d["y_prompt"][0, :, c], k.yst[:, n % 2, 0, :]).then_inc(k.y_stored[n % 2], 16)
            g.dma_start(d["y_sample"][0, :, c].rearrange("(b p) n -> p b n", p=P), k.yst[:, n % 2, 1:NB, :]
                        ).then_inc(k.y_stored[n % 2], 16)
        g.wait_ge(k.stored, 32)
        for n in range(2):
            g.wait_ge(k.y_stored[n], 32 * DT // 2)


def two_layers(nc, d):
    with ExitStack() as stack:
        k = Kernel(nc, d, stack)
        block = stack.enter_context(nc.Block())

        @block.sync
        def _(eng):
            Loads(k, eng).program()

        @block.tensor
        def _(eng):
            Products(k, eng).program()

        @block.scalar
        def _(eng):
            Activations(k, eng).program()

        @block.vector
        def _(eng):
            Elementwise(k, eng).program()

        @block.gpsimd
        def _(eng):
            Moves(k, eng).program()


def rope_tables():
    pairs, grid = ROPE // 4, 64
    inv = (1.0 / (np.float32(10000.0) ** (np.arange(pairs, dtype=np.float32) / np.float32(pairs)))
           ).astype(np.float32)
    n = np.arange(SMP)
    pos = np.stack([n // grid, n % grid]).astype(np.float32)
    out = np.zeros((2, P, TOK), np.float32)
    out[0] = 1.0
    for p in range(P):
        axis, half, i = p % ROPE // 32, p % 32 // 16, p % 16
        angle = (pos[axis] * inv[i]).astype(np.float32).astype(np.float64)
        out[0, p, CTX:] = np.cos(angle)
        out[1, p, CTX:] = np.sin(angle) * (1 if half else -1)
    return out


_INS = ["x_prompt", "x_sample", "cache_ckv", "cache_krope", "c", "c_ctx", "ada_w", "ada_b", "norm1_g",
        "norm2_g", "a_w_in", "a_v_g", "a_w_s", "a_b_s", "a_w_out", "b_w_dq", "b_q_g", "b_w_uq",
        "b_w_dkv", "b_kv_g", "b_w_ukv", "b_w_o", "f_w_in", "f_w_out", "final_g"]
_OUTS = [("y_prompt", (1, CTX, D)), ("y_sample", (1, SMP, D)), ("new_ckv", (1, 1, CTX, KVL)),
         ("new_krope", (1, 1, CTX, ROPE))]


def kernel(**inputs):
    import concourse.bacc as _bacc
    from concourse.bass_utils import run_bass_kernel_spmd as _run

    nc = _bacc.Bacc("TRN2", target_bir_lowering=False, num_devices=1)
    arrays = {f"in_{n}": np.ascontiguousarray(inputs[n]) for n in _INS}
    arrays["in_rope"] = rope_tables()
    arrays["in_ident"] = np.eye(P, dtype=np.float32)
    d = {n[3:]: nc.dram_tensor(n, a.shape, F32, kind="ExternalInput").ap() for n, a in arrays.items()}
    for name, shape in _OUTS:
        d[name] = nc.dram_tensor(name, shape, F32, kind="ExternalOutput").ap()
    two_layers(nc, d)
    r = _run(nc, [arrays], core_ids=[0])
    return tuple(r.results[0][name] for name, _ in _OUTS)
```

```python
import math
from contextlib import ExitStack, contextmanager

import numpy as np

import concourse.bass as bass
from concourse import mybir

F32 = mybir.dt.float32
F32R = mybir.dt.float32r
ACT = mybir.ActivationFunctionType
ALU = mybir.AluOpType
AX_X = mybir.AxisListType.X

P = 128
D = 1024
DT = D // P
CTX, SMP, PAST = 128, 1024, 256
TOK = CTX + SMP
NB = TOK // P
BANKS, CH = 3, TOK // 3
KEYS = TOK + PAST
AW = 2 * D
GT = AW // P
GROUPS = 8
FF = 2816
FT = FF // P
HEADS, NOPE, ROPE, VD = 8, 128, 64, 128
QL, KVL = 512, 256
QT, CT = QL // P, KVL // P
EPS = 1e-6
SCALE = 1.0 / math.sqrt(NOPE + ROPE)
ADA = 6 * DT
SH1, SC1, G1, SH2, SC2, G2 = (n * DT for n in range(6))
ADA_HEAD = 2 * DT
UNIT = 1024
R_COND, R_BIAS = 0, 2 * DT
V_N1, V_N2, V_AV, V_QG, V_KVG, V_FG, V_END = 0, 16, 32, 48, 52, 54, 62
T0_PROBS = 4 + 2 * NB + 3 * GT + 4
SWAP = [(p + 16) % 32 for p in range(32)]


class Count:

    def __init__(self, n=0):
        self.n, self.i, self.per = n, None, 0

    def at(self, off=0):
        v = self.n + off
        if self.i is None:
            return v
        assert v > 0
        return self.i * self.per + v

    def half(self, off=0):
        v = (self.n + off) // 2
        if self.i is None:
            return v
        assert v >= 0 and self.per % 2 == 0
        return self.i * (self.per // 2) + v

    def odd(self, off=0):
        return (self.n + off) % 2

    def past(self, n):
        return self.i is not None or self.n > n

    def step(self, k=1):
        self.n += k


def span(ps, lo, hi):
    if hi - lo <= CH:
        return ps[:, lo // CH, lo % CH:lo % CH + hi - lo]
    return ps[:, lo // CH:hi // CH, 0:CH]


PARTS = [(0, CTX, 0), (CTX, CH, 1), (CH, TOK, 1)]


@contextmanager
def repeat(eng, times, *streams):
    start = [c.n for c, _ in streams]
    with eng.Fori(0, times) as i:
        for c, per in streams:
            c.i, c.per = i, per
        yield i
    for (c, per), n in zip(streams, start):
        assert c.n == n + per, (c.n, n, per)
        c.n, c.i = n + per * times, None


class Kernel:

    def __init__(self, nc, d, stack):
        self.nc, self.d = nc, d
        top = [16640]

        def place(name, shape, dt=F32, offset=None):
            o = (top[0] if offset is None else offset) + 63 & ~63
            size = int(np.prod(shape[1:])) * 4
            if offset is None:
                top[0] = o + size
            assert o + size <= nc.sbuf_usable_end, (name, o + size)
            return nc.alloc_sbuf_tensor_at(name, shape, dt, offset=o)

        def region(start, *items):
            out = []
            for name, shape, dt in items:
                start = start + 63 & ~63
                out.append(place(name, shape, dt, start))
                start += int(np.prod(shape[1:])) * 4
            return out

        self.x = place("x", [P, DT, TOK])
        self.wraw = place("wraw", [P, 2, UNIT])
        self.whi = place("whi", [P, 2, UNIT], F32R)
        self.wlo = place("wlo", [P, 2, UNIT], F32R)
        tmp_at = top[0] + 63 & ~63
        self.tmp = place("tmp", [P, 4, TOK])
        acc_at = top[0] + 63 & ~63
        self.acc = place("acc", [P, TOK])
        self.rstd = place("rstd", [P, TOK])
        self.ident = place("ident", [P, P])
        self.ones = place("ones", [P, P])
        self.mod = place("mod", [P, 2 * ADA, 2])
        self.gain = place("gain", [P, DT, 2])
        self.vecs = place("vecs", [P, V_END])
        self.bias = place("bias", [P, 2 * ADA])
        self.cond = place("cond", [P, DT, 2])
        self.rv = place("rv", [P, NB])
        self.soft = place("soft", [P, 4, 2])
        self.nck = place("nck", [P, KVL + ROPE])
        rest = top[0] + 63 & ~63
        wide = [P, DT, TOK]
        self.xin, self.aldr, self.rowsa, self.rowsb, self.wsraw = region(
            rest, ("xin", [P, NB, D], F32), ("aldr", [P, 4, 2 * UNIT], F32),
            ("rowsa", [P, P], F32), ("rowsb", [P, P], F32), ("wsraw", [P, GROUPS, P], F32))
        self.hhi, self.hlo, self.ghi, self.glo = region(
            rest, ("hhi", wide, F32R), ("hlo", wide, F32R),
            ("ghi", [P, 2, TOK], F32R), ("glo", [P, 2, TOK], F32R))
        mid = rest + 2 * DT * TOK * 4
        self.vst, self.adv = region(mid, ("vst", [P, 2, TOK], F32), ("adv", [P, 2, UNIT], F32))
        late = mid + 4 * TOK * 4
        self.wst, self.bsb, self.vld, = region(
            late, ("wst", [P, GROUPS, P], F32), ("bsb", [P, GROUPS, P], F32), ("vld", [P, 2, TOK], F32))
        self.adu, = region(late + 2 * UNIT * 4 + 2 * TOK * 4, ("adu", [P, 2, UNIT], F32))
        keys = [P, CT, KEYS]
        self.ckh, self.ckl, self.krh, self.krl, self.ckf = region(
            mid, ("ckh", keys, F32R), ("ckl", keys, F32R), ("krh", [P, KEYS], F32R),
            ("krl", [P, KEYS], F32R), ("ckf", [P, CT, TOK], F32))
        after = mid + (2 * CT + 2) * KEYS * 4
        self.qah, self.qal, self.cs = region(
            rest, ("qah", [P, QT, TOK], F32R), ("qal", [P, QT, TOK], F32R), ("cs", [P, 2, TOK], F32))
        self.pa, = region(acc_at + TOK * 4, ("pa", [P, 2, 2, 2, P], F32))
        self.pah, = region(tmp_at + 2 * TOK * 4, ("pah", [P, 4, 2, 2, P], F32))
        self.csk, = region(acc_at, ("csk", [P, 2, TOK], F32))
        self.qnh, self.qnl, self.qrp, self.kth, self.ktl, self.vh, self.vl = region(
            rest, ("qnh", [P, TOK], F32R), ("qnl", [P, TOK], F32R), ("qrp", [P, TOK], F32R),
            ("kth", [P, KEYS], F32R), ("ktl", [P, KEYS], F32R),
            ("vh", [P, KEYS // P, 2, P], F32R), ("vl", [P, KEYS // P, 2, P], F32R))
        o = rest + (3 * TOK + 2 * KEYS + 4 * KEYS) * 4
        self.oh, self.ol = region(o, ("oh", [P, 2, TOK], F32R), ("ol", [P, 2, TOK], F32R))
        assert o + 4 * TOK * 4 <= mid, (o + 4 * TOK * 4, mid)
        row = [P, SMP + PAST]
        pr2, qld0, of0 = region(o + 4 * TOK * 4, ("pr2", row, F32), ("qld0", [P, CH], F32),
                                ("of0", [P, 2 * P], F32))
        assert o + 4 * TOK * 4 + (SMP + PAST + CH + 2 * P) * 4 <= mid
        self.cin, self.kin = region(tmp_at + 3 * TOK * 4, ("cin", [P, 2, KVL], F32), ("kin", [P, 2, P], F32))
        pr0, pr1, qld1 = region(after, ("pr0", row, F32), ("pr1", row, F32), ("qld1", [P, CH], F32))
        self.pth, self.ptl, self.qlr, qld2, of1 = region(
            tmp_at, ("pth", [P, 10, 2, P], F32R), ("ptl", [P, 10, 2, P], F32R), ("qlr", [P, TOK], F32),
            ("qld2", [P, CH], F32), ("of1", [P, 2 * P], F32))
        assert 4 * (2 * 10 * 2 * P + TOK + CH + 2 * P) <= 6 * TOK * 4
        self.pr, self.qld, self.of = (pr0, pr1, pr2), (qld0, qld1, qld2), (of0, of1)
        self.yst, = region(rest, ("yst", [P, 2, NB, P], F32))

        self.sets = [stack.enter_context(nc.psum_tensor(f"set{n}", [P, BANKS, 512], F32)) for n in range(2)]
        self.tps = [stack.enter_context(nc.psum_tensor(f"turned{n}", [P, 512], F32)) for n in range(2)]

        self.v_dram = nc.dram_tensor("v_scratch", [GT, P, TOK], F32, kind="Internal").ap()
        self.q_dram = nc.dram_tensor("q_scratch", [HEADS, 2, P, TOK], F32, kind="Internal").ap()

        def sem(name):
            return stack.enter_context(nc.semaphore(name))

        self.wload = [sem("unit_loaded_0"), sem("unit_loaded_1")]
        self.hi_done = sem("unit_hi_done")
        self.lo_done = sem("unit_lo_done")
        self.mm_done = sem("job_done")
        self.freed = [sem("set_freed_0"), sem("set_freed_1")]
        self.t_done = sem("turned")
        self.t_free = [sem("turned_freed_0"), sem("turned_freed_1")]
        self.sq_ready = sem("squares_ready")
        self.sq_used = sem("squares_summed")
        self.rs_ready = sem("mean_square_ready")
        self.diag_ready = sem("root_diagonals_ready")
        self.rt_ready = sem("rstd_ready")
        self.n_ready = sem("scaled_ready")
        self.hf_ready = sem("modulated_ready")
        self.hh_ready = sem("input_hi_ready")
        self.h_ready = sem("input_ready")
        self.af_ready = sem("hidden_ready")
        self.ah_ready = sem("hidden_hi_ready")
        self.a_ready = sem("hidden_parts_ready")
        self.in_loaded = [sem(f"input_loaded_{n}") for n in range(NB)]
        self.rows_loaded = sem("vector_rows_loaded")
        self.ws_loaded = sem("spatial_loaded")
        self.id_loaded = sem("identity_loaded")
        self.ones_set = sem("ones_set")
        self.al_loaded = [sem(f"ada_head_loaded_{n}") for n in range(4)]
        self.al_used = sem("ada_head_used")
        self.al_summed = sem("ada_head_summed")
        self.al_read = sem("ada_head_read")
        self.ad_loaded = [sem("ada_loaded_0"), sem("ada_loaded_1")]
        self.ad_summed = sem("ada_summed")
        self.spilled = [sem("v_spilled_0"), sem("v_spilled_1")]
        self.v_loaded = [sem("v_loaded_0"), sem("v_loaded_1")]
        self.vs_ready = sem("v_scaled")
        self.rope_loaded = sem("rope_loaded")
        self.cache_loaded = sem("cache_loaded")
        self.ck_ready = sem("keys_ready")
        self.q_spilled = [sem(f"q_spilled_{n}") for n in range(4)]
        self.qf_ready = sem("q_rope_ready")
        self.q_loaded = sem("q_loaded")
        self.qh_ready = sem("q_hi_ready")
        self.q_ready = sem("q_ready")
        self.kh_ready = sem("kv_hi_ready")
        self.nb_ready = sem("max_ready")
        self.inv_ready = sem("inverse_sums_ready")
        self.p_ready = sem("probs_ready")
        self.pth_ready = sem("probs_turned_hi")
        self.of_ready = sem("head_out_read")
        self.oh_ready = sem("head_out_hi")
        self.o_ready = sem("head_out_ready")
        self.dv_step = sem("vector_step")
        self.ac_step = sem("scalar_step")
        self.y_ready = sem("y_tile_ready")
        self.stored = sem("outputs_stored")
        self.y_stored = [sem("y_stored_0"), sem("y_stored_1")]


class Engine:

    def __init__(self, k, eng):
        self.k, self.eng, self.nc = k, eng, k.nc
        self.J = Count()
        self.U = Count()
        self.T = Count()
        self.Q = Count()
        self.R = Count()
        self.H = Count()
        self.A = Count()
        self.V = Count()
        self.K = Count()
        self.F = Count()
        self.S = Count()
        self.G = Count()
        self.B = Count()
        self.O = Count()
        self.L = Count()
        self.E = Count()
        self.W = Count()
        self.loaded = [Count(), Count()]


def tiles(w, dims, k):
    return w.rearrange("(k p) n -> p k n", p=P)


class Loads(Engine):
    def unit(self, halves):
        k, s = self.k, self.U.odd()
        if self.U.past(1):
            self.eng.wait_ge(k.lo_done, self.U.at(-1))
        for lo, n, src in halves:
            self.eng.dma_start(k.wraw[:, s, lo:lo + n].rearrange("p (k c) -> p k c", c=src.shape[-1]), src
                               ).then_inc(k.wload[s], 16)
        self.U.step()

    def in_unit(self, w, col):
        v = w.rearrange("(k p) n -> p k n", p=P)
        self.unit([(n * 512, 512, v[:, 4 * n:4 * n + 4, bass.ds(col, P)]) for n in range(2)])

    def out_unit(self, w, row, half):
        self.unit([(n * 512, 512, w[bass.ds(row + n * P, P), half * 512:half * 512 + 512]
                    .rearrange("p (a c) -> p a c", a=1)) for n in range(2)])

    def ada_tiles(self, raw, layer, tile):
        k = self.k
        if self.V.past(1):
            self.eng.wait_ge(k.ad_summed, self.V.at(-1))
        v = k.d["ada_w"][layer].rearrange("(k p) n -> p k n", p=P)
        for u, slot in enumerate(raw):
            self.eng.dma_start(slot.rearrange("p (k c) -> p k c", c=P),
                               v[:, :, bass.ds((tile + u) * P, P)]).then_inc(k.ad_loaded[self.V.odd()], 16)
        self.V.step()

    def ada_job(self, n, tile):
        k = self.k
        self.ada_tiles([k.adu[:, 0, :], k.adu[:, 1, :]] if n == 2 else [k.tmp[:, 3, 0:UNIT]], 1, tile)

    def program(self):
        k, d, sp, J = self.k, self.k.d, self.eng, self.J
        sp.dma_start(k.ident[:], d["ident"]).then_inc(k.id_loaded, 16)
        sp.dma_start(k.rowsa[0:8, :], d["c_ctx"].rearrange("(a b) -> a b", b=P)).then_inc(k.rows_loaded, 16)
        sp.dma_start(k.rowsa[8:16, :], d["c"][0].rearrange("(a b) -> a b", b=P)).then_inc(k.rows_loaded, 16)
        sp.dma_start(k.rowsa[16:16 + 2 * ADA, :], d["ada_b"].rearrange("l (a b) -> (l a) b", b=P)
                     ).then_inc(k.rows_loaded, 16)
        for lo, name in ((V_N1, "norm1_g"), (V_N2, "norm2_g"), (V_AV, "a_v_g"), (V_QG, "b_q_g"),
                         (V_KVG, "b_kv_g")):
            src = d[name].rearrange("l (a b) -> (l a) b", b=P)
            sp.dma_start(k.rowsb[lo:lo + src.shape[0], :], src).then_inc(k.rows_loaded, 16)
        sp.dma_start(k.rowsb[V_FG:V_END, :], d["final_g"].rearrange("(a b) -> a b", b=P)
                     ).then_inc(k.rows_loaded, 16)
        for b in range(NB):
            src = d["x_prompt"][0] if b == 0 else d["x_sample"][0, (b - 1) * P:b * P, :]
            sp.dma_start(k.xin[:, b, :], src).then_inc(k.in_loaded[b], 16)
            if b == 0:
                sp.dma_start(k.wsraw[:], d["a_w_s"][0].rearrange("g p q -> p g q")).then_inc(k.ws_loaded, 16)
                sp.dma_start(k.bsb[:].rearrange("p g q -> p (g q)"),
                             d["a_b_s"].rearrange("l g q -> l (g q)").partition_broadcast(P)
                             .rearrange("p a n -> p (a n)")).then_inc(k.ws_loaded, 16)
        first = d["ada_w"][0].rearrange("(k p) n -> p k n", p=P)
        for n in range(ADA_HEAD // 2):
            if n >= 4 and n % 2 == 0:
                sp.wait_ge(k.al_used, (n - 2) // 2)
            elif n >= 4:
                sp.wait_ge(k.al_summed, (n - 3) // 2)
            sp.dma_start(k.aldr[:, n % 4, :].rearrange("p (k c) -> p k c", k=DT),
                         first[:, :, n * 256:n * 256 + 256]).then_inc(k.al_loaded[n % 4], 16)
        w_in = d["a_w_in"][0]
        self.in_unit(w_in, AW)
        self.in_unit(w_in, AW + P)
        slots = [[w[:, u, :] for u in range(2)] for w in (k.adv, k.adu)]
        for h in range(2):
            self.ada_tiles(slots[h], 0, ADA_HEAD + 2 * h)
        with repeat(sp, GT // 2 - 1, (self.U, 2), (self.V, 2)) as i:
            for h in range(2):
                self.in_unit(w_in, AW + (2 * i + 2 + h) * P)
                self.ada_tiles(slots[h], 0, ADA_HEAD + 4 + 4 * i + 2 * h)
        for h in range(2):
            self.in_unit(w_in, h * P)
        sp.wait_ge(k.ad_summed, self.V.n)
        self.ada_job(2, 0)
        sp.wait_ge(k.sq_used, DT + GT)
        with repeat(sp, GT // 2 - 1, (self.U, 4), (self.V, 4)) as i:
            self.mixer_turn(i, False)
        self.mixer_turn(GT // 2 - 1, True)
        self.ffn(0)
        self.attention()
        self.ffn(1)

    def mixer_turn(self, i, last):
        k, d = self.k, self.k.d
        w_in, w_out = d["a_w_in"][0], d["a_w_out"][0]
        if not last:
            self.in_unit(w_in, (2 * i + 2) * P)
        self.ada_job(1, 6 * i + 2)
        self.ada_job(2, 6 * i + 3)
        self.out_unit(w_out, 2 * P * i, 0)
        self.out_unit(w_out, 2 * P * i, 1)
        if last:
            self.in_unit(d["f_w_in"][0], 0)
        else:
            self.in_unit(w_in, (2 * i + 3) * P)
        self.ada_job(1, 6 * i + 5)
        if last:
            self.in_unit(d["f_w_in"][0], FF)
        else:
            self.ada_job(2, 6 * i + 6)

    def ffn_turn(self, layer, i, last):
        w_in, w_out = self.k.d["f_w_in"][layer], self.k.d["f_w_out"][layer]
        self.in_unit(w_in, FF + (2 * i + 1) * P)
        if not last:
            self.in_unit(w_in, (2 * i + 2) * P)
        self.out_unit(w_out, 2 * P * i, 0)
        self.out_unit(w_out, 2 * P * i, 1)
        if not last:
            self.in_unit(w_in, FF + (2 * i + 2) * P)
            self.in_unit(w_in, (2 * i + 3) * P)

    def ffn(self, layer):
        self.in_unit(self.k.d["f_w_in"][layer], P)
        with repeat(self.eng, FT // 2 - 1, (self.U, 6)) as i:
            self.ffn_turn(layer, i, False)
        self.ffn_turn(layer, FT // 2 - 1, True)

    def attention(self):
        k, d = self.k, self.k.d
        w_dq, w_uq, w_dkv = d["b_w_dq"][0], d["b_w_uq"][0], d["b_w_dkv"][0]
        v = w_dkv.rearrange("(k p) n -> p k n", p=P)
        self.unit([(n * 256, 256, v[:, 4 * n:4 * n + 4, KVL:KVL + ROPE]) for n in range(2)])
        for m in range(CT):
            self.in_unit(w_dkv, m * P)
        for m in range(QT):
            self.in_unit(w_dq, m * P)
        q = w_uq.rearrange("(k p) (h c) -> p k h c", p=P, c=NOPE + ROPE)
        with repeat(self.eng, HEADS // 2, (self.U, 2)) as i:
            self.unit([(h * 512, 512, q[:, :, 2 * i + h, 0:NOPE]) for h in range(2)])
            self.unit([(h * 256, 256, q[:, :, 2 * i + h, NOPE:]) for h in range(2)])
        kv = d["b_w_ukv"][0].rearrange("(k p) (h c) -> p k h c", p=P, c=NOPE + VD)
        with repeat(self.eng, HEADS // 2, (self.U, 4)) as i:
            for part in range(2):
                self.unit([(n * 256, 256, kv[:, n, bass.ds(2 * i, 2), part * P:part * P + P])
                           for n in range(CT)])
            self.out_unit(d["b_w_o"][0], 2 * P * i, 0)
            self.out_unit(d["b_w_o"][0], 2 * P * i, 1)
        self.in_unit(d["f_w_in"][1], 0)
        self.in_unit(d["f_w_in"][1], FF)


class Products(Engine):
    def open(self):
        k = self.k
        if self.J.past(1):
            self.eng.wait_ge(k.freed[self.J.odd()], self.J.half())
        return k.sets[self.J.odd()]

    def close(self, last):
        last.then_inc(self.k.mm_done, 1)
        self.J.step()

    def unit_ready(self, off=0):
        self.eng.wait_ge(self.k.lo_done, self.U.at(1 + off))

    def parts(self, ps, weights, moving, cols=CH, inputs_ready=None):
        nc, n, last = self.nc, len(weights), None
        for i in range(n):
            if inputs_ready is not None:
                self.eng.wait_ge(self.k.h_ready, inputs_ready + i + 1)
            (wh, wl), (mh, ml) = weights[i], moving[i]
            for p, (w, m) in enumerate(((wh, mh), (wh, ml), (wl, mh))):
                for b in range(BANKS):
                    last = nc.tensor.matmul(ps[:, b, 0:cols], w, m[:, b * cols:(b + 1) * cols],
                                            start=(i == 0 and p == 0), stop=(i == n - 1 and p == 2))
        return last

    def weight(self, slot, at):
        k = self.k
        return k.whi[:, slot, at:at + P], k.wlo[:, slot, at:at + P]

    def in_job(self, first=False):
        k, s = self.k, self.U.odd()
        ps = self.open()
        self.unit_ready()
        self.close(self.parts(ps, [self.weight(s, n * P) for n in range(DT)],
                              [(k.hhi[:, n, :], k.hlo[:, n, :]) for n in range(DT)],
                              inputs_ready=self.H.n if first else None))
        if first:
            self.H.step(DT)
        self.U.step()

    def first_in_jobs(self):
        k, nc, J = self.k, self.nc, self.J
        self.unit_ready(1)
        ps = [self.open()]
        self.eng.wait_ge(k.freed[J.odd(1)], J.half(1))
        ps.append(k.sets[J.odd(1)])
        slots = (self.U.odd(), self.U.odd(1))
        for n in range(DT):
            self.eng.wait_ge(k.h_ready, self.H.n + n + 1)
            for t in range(2):
                wh, wl = self.weight(slots[t], n * P)
                for p, (w, m) in enumerate(((wh, k.hhi), (wh, k.hlo), (wl, k.hhi))):
                    for b in range(BANKS):
                        last = nc.tensor.matmul(ps[t][:, b, 0:CH], w, m[:, n, b * CH:(b + 1) * CH],
                                                start=(n == 0 and p == 0), stop=(n == DT - 1 and p == 2))
                if n == DT - 1:
                    self.close(last)
        self.H.step(DT)
        self.U.step(2)

    def out_jobs(self, mh, ml, ready, count):
        s = self.U.odd()
        self.unit_ready()
        if ready is not None:
            self.eng.wait_ge(ready, count)
        for n in range(DT // 2):
            ps = self.open()
            self.close(self.parts(ps, [self.weight(s, a * 512 + n * P) for a in range(2)],
                                  [(mh[:, a, :], ml[:, a, :]) for a in range(2)]))
        self.U.step()

    def ada_job(self, n):
        k, nc, b = self.k, self.nc, self.V.odd()
        ps = self.open()
        self.V.step()
        self.eng.wait_ge(k.ad_summed, self.V.at())
        for u in range(n):
            for c in range(2):
                last = nc.tensor.matmul(ps[:, 0, 2 * u + c:2 * u + c + 1], k.pa[:, b, u, c, :],
                                        k.ones[:, 0:1], start=True, stop=True)
        self.close(last)

    def turn(self, sources, width=P):
        k, nc, b = self.k, self.nc, self.T.odd()
        if self.T.past(1):
            self.eng.wait_ge(k.t_free[b], self.T.half())
        for n, src in enumerate(sources):
            rows = src.shape[0]
            last = nc.tensor.transpose(k.tps[b][0:src.shape[-1], n * width:n * width + rows], src,
                                       k.ident[0:rows, 0:rows])
        last.then_inc(k.t_done, 1)
        self.T.step()

    def statistics(self):
        k, nc = self.k, self.nc
        self.column_sums()
        ps = self.open()
        self.R.step()
        self.eng.wait_ge(k.diag_ready, self.R.at())
        for b in range(NB):
            last = nc.tensor.matmul(ps[:, b // 3, b % 3 * P:(b % 3 + 1) * P], k.ones[:],
                                    k.acc[:, b * P:(b + 1) * P], start=True, stop=True)
        self.close(last)

    def column_sums(self):
        k, nc = self.k, self.nc
        ps = self.open()
        self.eng.wait_ge(k.sq_used, self.Q.at())
        for b in range(NB):
            last = nc.tensor.matmul(ps[:, 0, b:b + 1], k.acc[:, b * P:(b + 1) * P], k.ones[:, 0:1],
                                    start=True, stop=True)
        self.close(last)

    def program(self):
        k, pe, nc = self.k, self.eng, self.nc
        pe.wait_ge(k.id_loaded, 16)
        pe.wait_ge(k.rows_loaded, 16 * 9)
        self.turn([k.rowsa[0:2 * DT + 2 * ADA, :]])
        self.turn([k.rowsb[0:V_END, :]])
        pe.wait_ge(k.ws_loaded, 32)
        for n in range(2):
            self.turn([k.wsraw[:, 4 * n + g, :] for g in range(4)])
        for b in range(NB):
            pe.wait_ge(k.in_loaded[b], 16)
            for n in range(2):
                self.turn([k.xin[:, b, (4 * n + f) * P:(4 * n + f + 1) * P] for f in range(4)])
        pe.wait_ge(k.ones_set, 1)
        self.Q.step(DT)
        self.statistics()
        pe.wait_ge(k.freed[0], 1)
        pe.wait_ge(k.t_free[0], 1)
        ps = k.sets[0]
        for n in range(0, ADA_HEAD // 2, 2):
            pe.wait_ge(k.al_loaded[n % 4], 16 * (n // 4 + 1))
            for u in range(2):
                for i in range(DT):
                    c = 4 * n + 2 * u
                    last = nc.tensor.matmul(ps[:, 0, c:c + 2],
                                            k.aldr[:, n % 4, i * 256 + u * P:i * 256 + (u + 1) * P],
                                            k.cond[:, i, :], start=(i == 0), stop=(i == DT - 1))
            last.then_inc(k.al_used, 1)
        for n in range(1, ADA_HEAD // 2, 2):
            pe.wait_ge(k.al_summed, n // 2 + 1)
            for u in range(2):
                for c in range(2):
                    o = 4 * n + 2 * u + c
                    last = nc.tensor.matmul(ps[:, 0, o:o + 1], k.pah[:, n // 2, u, c, :], k.ones[:, 0:1],
                                            start=True, stop=True)
            last.then_inc(k.al_used, 1)
        pe.wait_ge(k.al_read, 1)
        self.mixer()
        self.ffn()
        self.attention()
        self.ffn()
        self.Q.step(DT)
        self.statistics()
        for n in range(DT):
            pe.wait_ge(k.y_ready, n + 1)
            for g in range(3):
                self.turn([k.tmp[:, n % 4, (3 * g + b) * P:(3 * g + b + 1) * P] for b in range(3)])

    def mixer(self):
        k, pe, nc, J, T = self.k, self.eng, self.nc, self.J, self.T

        def v_tile(m_even, first=False):
            self.in_job(first)
            self.ada_job(2)
            pe.wait_ge(k.freed[J.odd(-2)], J.half(-2) + 1)
            for g in range(3):
                self.turn([k.tmp[:, m_even, (3 * g + b) * P:(3 * g + b + 1) * P] for b in range(3)])

        v_tile(0, first=True)
        v_tile(1)
        with repeat(pe, GT // 2 - 1, (J, 4), (T, 6), (self.U, 2), (self.V, 2)):
            v_tile(0)
            v_tile(1)
        self.Q.step(GT)
        self.column_sums()
        self.in_job()
        with repeat(pe, GT // 2 - 1, (J, 16), (self.U, 4), (self.V, 4), (self.A, 2)) as i:
            self.mixer_turn(i, False)
        self.mixer_turn(GT // 2 - 1, True)

    def mix(self, i, m):
        k, nc = self.k, self.nc
        ps = self.open()
        self.eng.wait_ge(k.vs_ready, self.A.at(m + 1))
        for b in range(NB):
            last = nc.tensor.matmul(ps[:, b // 3, b % 3 * P:(b % 3 + 1) * P],
                                    k.vld[:, m, b * P:(b + 1) * P], k.wst[:, i, :],
                                    start=True, stop=True)
        self.close(last)

    def mixer_turn(self, i, last):
        k = self.k
        self.mix(i, 0)
        self.ada_job(2)
        self.in_job()
        self.mix(i, 1)
        self.ada_job(1)
        self.ada_job(2)
        if not last:
            self.in_job()
        self.ada_job(1)
        self.A.step(2)
        self.out_jobs(k.ghi, k.glo, k.a_ready, self.A.at())
        self.out_jobs(k.ghi, k.glo, None, None)

    def ffn_turn(self, first, last):
        k = self.k
        for _ in range(3 if last or first else 4):
            self.in_job()
        self.A.step(2)
        self.out_jobs(k.ghi, k.glo, k.a_ready, self.A.at())
        self.out_jobs(k.ghi, k.glo, None, None)

    def ffn(self):
        self.Q.step(DT)
        self.statistics()
        self.first_in_jobs()
        self.ffn_turn(True, False)
        with repeat(self.eng, FT // 2 - 2, (self.J, 12), (self.U, 6), (self.A, 2)):
            self.ffn_turn(False, False)
        self.ffn_turn(False, True)

    def attention(self):
        k, pe, nc, J = self.k, self.eng, self.nc, self.J
        self.Q.step(DT)
        self.statistics()
        self.first_in_jobs()
        self.in_job()
        pe.wait_ge(k.cache_loaded, 48)
        self.turn([k.cin[:, b, m * P:(m + 1) * P] for m in range(CT) for b in range(2)])
        self.turn([k.kin[:, b, :] for b in range(2)])
        self.in_job()
        pe.wait_ge(k.ck_ready, 1)
        self.turn([k.tmp[0:ROPE, 2, 0:CTX]])
        self.Q.step(CT)
        self.statistics()
        for _ in range(QT - 1):
            self.in_job()
        pe.wait_ge(k.ck_ready, 3)
        self.turn([k.ckf[:, m, 0:CTX] for m in range(CT)])
        self.Q.step(QT)
        self.statistics()
        pe.wait_ge(k.h_ready, self.H.n + QT)
        self.H.step(QT)
        with repeat(pe, HEADS // 2, (J, 4), (self.U, 2)):
            for _ in range(2):
                s = self.U.odd()
                self.unit_ready()
                for h in range(2):
                    ps = self.open()
                    self.close(self.parts(ps, [self.weight(s, (4 * h + n) * P) for n in range(QT)],
                                          [(k.qah[:, n, :], k.qal[:, n, :]) for n in range(QT)]))
                self.U.step()
        with repeat(pe, HEADS // 2, (J, 34), (self.U, 4), (self.T, 50), (self.G, 2),
                    (self.B, 18), (self.O, 10)):
            self.head_pair()

    KEY_CH = ((0, 480), (480, 944), (944, KEYS))

    def keys_job(self, h, s):
        k, nc = self.k, self.nc
        ps = self.open()
        for n in range(CT):
            wh, wl = self.weight(s, (2 * n + h) * P)
            for p, (w, m) in enumerate(((wh, k.ckh), (wh, k.ckl), (wl, k.ckh))):
                for b, (lo, hi) in enumerate(self.KEY_CH):
                    last = nc.tensor.matmul(ps[:, b, 0:hi - lo], w, m[:, n, lo:hi],
                                            start=(n == 0 and p == 0), stop=(n == CT - 1 and p == 2))
        self.close(last)

    def values_job(self, blocks, s):
        k, nc = self.k, self.nc
        ps = self.open()
        for i, b in enumerate(blocks):
            for n in range(CT):
                wh, wl = (w[:, s, n * 256:(n + 1) * 256] for w in (k.whi, k.wlo))
                for p, (c, w) in enumerate(((k.ckh, wh), (k.ckh, wl), (k.ckl, wh))):
                    last = nc.tensor.matmul(ps[:, i // 2, i % 2 * 256:(i % 2 + 1) * 256],
                                            c[:, n, b * P:(b + 1) * P], w,
                                            start=(n == 0 and p == 0), stop=(n == CT - 1 and p == 2))
        self.close(last)

    def scores(self, ps, b, between=None):
        k, nc, c = self.k, self.nc, slice(b * P, (b + 1) * P)
        chunks = ((0, 0, CTX),) if b == 0 else ((0, CTX, 512), (1, CTX + 512, 512), (2, CTX + 1024, 256))
        passes = ((k.qnh, k.kth), (k.qnh, k.ktl), (k.qnl, k.kth), (k.qrp, k.krh), (k.qrp, k.krl))
        for p, (q, key) in enumerate(passes):
            if p == 3 and between is not None:
                self.turn_probs(between, True)
            for bank, lo, n in chunks:
                last = nc.tensor.matmul(ps[:, bank, 0:n], q[:, c], key[:, lo:lo + n],
                                        start=p == 0, stop=p == len(passes) - 1)
        return last

    def weighted(self, ps, h, pair):
        k, nc = self.k, self.nc
        blocks = range(1) if pair is None else range(1, KEYS // P)
        n = P if pair is None else 2 * P
        for i, b in enumerate(blocks):
            for p, (v, pt) in enumerate(((k.vh, k.pth), (k.vh, k.ptl), (k.vl, k.pth))):
                m = pt[:, i, :, :].rearrange("p a c -> p (a c)")[:, 0:n]
                last = nc.tensor.matmul(ps[:, 2, 256:256 + n], v[:, b, h, :], m,
                                        start=(i == 0 and p == 0), stop=(i == len(blocks) - 1 and p == 2))
        return last

    def probs_turned(self):
        self.eng.wait_ge(self.k.t_free[self.T.odd(-1)], self.T.half(-1) + 1)

    def turn_probs(self, s, rest):
        k = self.k
        self.eng.wait_ge(k.p_ready, self.B.at(s + 1))
        for lo, hi in prob_groups(s, rest):
            self.turn([k.pr[s % 3][:, b * P:(b + 1) * P] for b in range(lo, hi)])

    def head_pair(self):
        k, pe = self.k, self.eng
        ku, vu = self.U.odd(), self.U.odd(1)
        self.unit_ready()
        for h in range(2):
            if h == 0:
                self.keys_job(0, ku)
                self.unit_ready(1)
                self.values_job(range(0, 6), vu)
                self.values_job(range(6, 11), vu)
            else:
                self.U.step(2)
            self.G.step()
            pe.wait_ge(k.q_ready, self.G.at())
            for s in range(-2, 9):
                job, late = s + 2 < 9, s - 1 if s >= 1 else None
                if job:
                    ps = self.open()
                    last = self.scores(ps, (s + 3) % 9, late)
                else:
                    self.turn_probs(late, True)
                if s >= 2 and s % 2 == 0:
                    if not job:
                        ps = self.open()
                    self.probs_turned()
                    last = self.weighted(ps, h, s // 2 - 1)
                    job = True
                if job:
                    self.close(last)
                if s >= 0:
                    self.turn_probs(s, False)
                if s == 7 and h == 0:
                    self.keys_job(1, ku)
            ps = self.open()
            self.probs_turned()
            self.close(self.weighted(ps, h, None))
            self.B.step(9)
            self.O.step(5)
        self.out_jobs(k.oh, k.ol, k.o_ready, self.O.at())
        self.out_jobs(k.oh, k.ol, None, None)


class Activations(Engine):
    def act(self, out, in_, func=ACT.Copy, **kw):
        return self.nc.scalar.activation(out, in_, func, **kw)

    def split(self, double=False, first=False):
        k, s = self.k, self.U.odd()
        self.eng.wait_ge(k.wload[s], self.U.half() * 32 + 32)
        if not first:
            self.eng.wait_ge(k.mm_done, self.J.at())
        if double:
            o = k.whi[:, s, :].rearrange("p (k a c) -> p k a c", a=2, c=ROPE)
            i = k.wraw[:, s, 0:512].rearrange("p (k a c) -> p k a c", a=1, c=ROPE
                                              ).to_broadcast([P, DT, 2, ROPE])
        else:
            o, i = k.whi[:, s, :], k.wraw[:, s, :]
        self.act(o, i).then_inc(k.hi_done, 1)
        self.U.step()

    def squares(self, src):
        k = self.k
        if self.Q.past(1):
            self.eng.wait_ge(k.sq_used, self.Q.at(-1))
        self.act(k.tmp[:, 2 + self.Q.odd(), :], src, ACT.Square).then_inc(k.sq_ready, 1)
        self.Q.step()

    def root(self, out):
        self.eng.wait_ge(self.k.rs_ready, self.R.at(1))
        self.act(out, out, ACT.Sqrt).then_inc(self.k.rt_ready, 1)
        self.R.step()

    def roots(self, squared):
        k = self.k
        for n in range(0 if squared else DT):
            self.squares(k.x[:, n, :])
        self.J.step()
        self.root(k.rv[:])
        self.J.step()

    def norm(self, shift, squared=False, rooted=False):
        k, a = self.k, self.eng
        if not rooted:
            self.roots(squared)
        for n in range(DT):
            src, hf = k.tmp[:, n % 2, :], k.tmp[:, 2 + n % 2, :]
            a.wait_ge(k.n_ready, self.H.n + n + 1)
            if self.H.n + n >= 2:
                a.wait_ge(k.h_ready, self.H.n + n - 1)
            for lo, hi, c in ((0, CTX, 0), (CTX, TOK, 1)):
                self.act(hf[:, lo:hi], src[:, lo:hi], ACT.Identity, scale=k.gain[:, n, c:c + 1],
                         bias=k.mod[:, shift + n, c:c + 1]).then_inc(k.hf_ready, 1)
            a.wait_ge(k.hf_ready, 2 * (self.E.n + n + 1))
            self.act(k.hhi[:, n, :], hf).then_inc(k.hh_ready, 1)
        self.H.step(DT)
        self.E.step(DT)

    def program(self):
        k, a, T = self.k, self.eng, self.T
        a.wait_ge(k.t_done, 1)
        for c in range(2):
            self.act(k.cond[:, :, c], k.tps[0][:, c * DT:(c + 1) * DT], ACT.Silu)
        self.act(k.bias[:], k.tps[0][:, 2 * DT:2 * DT + 2 * ADA]).then_inc(k.t_free[0], 1)
        a.wait_ge(k.t_done, 2)
        self.act(k.vecs[:], k.tps[1][:, 0:V_END]).then_inc(k.t_free[1], 1)
        for n in range(NB):
            a.wait_ge(k.t_done, 4 + 2 * n + 1)
            self.act(k.x[:, 0:4, n * P:(n + 1) * P], k.tps[0][:].rearrange("p (f c) -> p f c", f=4)
                     ).then_inc(k.t_free[0], 1)
        T.step(4 + 2 * NB)
        a.wait_ge(k.t_free[0], 2 + NB)
        a.wait_ge(k.t_free[1], 2 + NB)
        self.roots(False)
        self.split(first=True)
        self.split(first=True)
        a.wait_ge(k.al_read, 1)
        self.mixer()
        self.ffn(0)
        self.attention()
        self.ffn(1)
        self.J.step()
        self.root(k.rv[:])
        self.J.step()

    def gelu(self, dst):
        k = self.k
        self.eng.wait_ge(k.mm_done, self.J.at(1))
        ps = k.sets[self.J.odd()]
        self.act(dst.rearrange("p (b c) -> p b c", b=BANKS), ps[:, :, 0:CH], ACT.Gelu
                 ).then_inc(k.freed[self.J.odd()], 1)
        self.J.step()

    def hidden_hi(self, h):
        k = self.k
        self.A.step()
        self.act(k.ghi[:, h, :], k.tmp[:, 1, :]).then_inc(k.ah_ready, 1)

    def mixer(self):
        k, a, J = self.k, self.eng, self.J
        self.norm(SH1, rooted=True)
        with repeat(a, GT // 2, (J, 4), (self.U, 2), (self.Q, 2)):
            for h in range(2):
                self.gelu(k.tmp[:, h, :])
                self.eng.wait_ge(k.freed[self.J.odd(-1)], self.J.half(-1) + 1)
                self.squares(k.tmp[:, h, :])
                self.split()
                J.step()
        self.T.step(3 * GT)
        J.step()
        self.root(k.rv[:])
        self.gelu(k.tmp[:, 0, :])
        self.split()
        with repeat(a, GT // 2 - 1, (J, 16), (self.U, 4), (self.A, 2)) as i:
            self.mixer_turn(i, False)
        self.mixer_turn(GT // 2 - 1, True)

    def mixed(self, i, m):
        k = self.k
        self.eng.wait_ge(k.mm_done, self.J.at(1))
        ps = k.sets[self.J.odd()]
        gain = k.vecs[:, V_AV:V_AV + GT].rearrange("p (g m) -> p g m", m=2)
        self.act(k.tmp[:, 2, :].rearrange("p (b c) -> p b c", b=BANKS), ps[:, :, 0:CH], ACT.Copy,
                 scale=gain[:, i, m:m + 1]).then_inc(k.freed[self.J.odd()], 1)
        self.J.step()
        self.eng.wait_ge(k.af_ready, self.A.at(1))
        self.hidden_hi(m)

    def mixer_turn(self, i, last):
        k, J = self.k, self.J
        self.mixed(i, 0)
        J.step()
        self.gelu(k.tmp[:, 0, :])
        self.split()
        self.mixed(i, 1)
        J.step(2)
        if not last:
            self.gelu(k.tmp[:, 0, :])
            self.split()
        J.step()
        if last:
            self.eng.wait_ge(k.ad_summed, GT + 4 * (GT // 2))
        self.out_tiles(0, last)
        self.split()
        self.out_tiles(1, last)
        self.split()

    def out_tiles(self, half, final):
        k, J = self.k, self.J
        for n in range(half * 4, half * 4 + 4):
            J.step()
            if final:
                self.eng.wait_ge(k.freed[J.odd(-1)], J.half(-1) + 1)
                self.squares(k.x[:, n, :])

    def gate(self):
        k = self.k
        self.eng.wait_ge(k.mm_done, self.J.at(1))
        ps = k.sets[self.J.odd()]
        self.act(k.tmp[:, 0, :].rearrange("p (b c) -> p b c", b=BANKS), ps[:, :, 0:CH], ACT.Silu
                 ).then_inc(k.freed[self.J.odd()], 1)
        self.J.step()

    def up(self, h):
        k = self.k
        self.J.step()
        self.eng.wait_ge(k.freed[self.J.odd(-1)], self.J.half(-1) + 1)
        self.hidden_hi(h)

    def ffn_turn(self, last, doubled=None):
        k, J = self.k, self.J
        self.up(0)
        self.split()
        self.gate()
        self.split()
        self.up(1)
        self.split()
        if not last:
            self.gate()
            self.split()
        self.out_tiles(0, last)
        if not last or doubled is not None:
            self.split(double=bool(doubled))
        self.out_tiles(1, last)
        if not last or doubled is not None:
            self.split()

    def ffn(self, layer):
        k = self.k
        if layer == 1:
            self.eng.wait_ge(k.freed[self.J.odd(-1)], self.J.half(-1) + 1)
            self.eng.wait_ge(k.freed[self.J.odd(-2)], self.J.half(-2) + 1)
        self.norm(layer * ADA + SH2, squared=layer == 0)
        self.gate()
        self.split()
        with repeat(self.eng, FT // 2 - 1, (self.J, 12), (self.U, 6), (self.A, 2)):
            self.ffn_turn(False)
        self.ffn_turn(True, doubled=True if layer == 0 else None)

    def wide(self, dst):
        k = self.k
        self.eng.wait_ge(k.mm_done, self.J.at(1))
        ps = k.sets[self.J.odd()]
        r = self.act(dst.rearrange("p (b c) -> p b c", b=BANKS), ps[:, :, 0:CH])
        r.then_inc(k.freed[self.J.odd()], 1)
        self.J.step()

    def attention(self):
        k, a, J, T = self.k, self.eng, self.J, self.T
        self.norm(ADA + SH1, True)
        a.wait_ge(k.h_ready, self.H.n)
        self.wide(k.tmp[:, 0, :])
        self.split()
        a.wait_ge(k.ck_ready, 1)
        self.act(k.krh[:, 0:TOK], k.tmp[:, 2, :]).then_inc(k.kh_ready, 1)
        for m in range(CT):
            self.wide(k.ckf[:, m, :])
            self.split()
        a.wait_ge(k.t_done, T.at(1))
        self.act(k.ckh[:, :, TOK:], k.tps[T.odd()][:, 0:CT * PAST].rearrange("p (m c) -> p m c", m=CT)
                 ).then_inc(k.kh_ready, 1)
        T.step()
        a.wait_ge(k.t_done, T.at(1))
        self.act(k.krh[:, TOK:], k.tps[T.odd()][:, 0:PAST]).then_inc(k.kh_ready, 1)
        T.step(2)
        self.wide(k.tmp[:, 0, :])
        self.split()
        self.Q.step(CT)
        J.step()
        self.root(k.rv[:])
        self.J.step()
        for m in range(CT):
            a.wait_ge(k.ck_ready, 2 + m)
            self.act(k.ckh[:, m, 0:TOK], k.ckf[:, m, :]).then_inc(k.kh_ready, 1)
        T.step()
        for m in range(1, QT):
            self.wide(k.tmp[:, m, :])
            if m < QT - 1:
                self.split()
            else:
                self.split(double=True)
        self.Q.step(QT)
        J.step()
        self.root(k.rv[:])
        self.J.step()
        for m in range(QT):
            a.wait_ge(k.n_ready, self.H.n + m + 1)
            self.act(k.qah[:, m, :], k.tmp[:, m, :]).then_inc(k.hh_ready, 1)
        self.H.step(QT)
        a.wait_ge(k.h_ready, self.H.n)
        self.queries(True, False)
        with repeat(a, HEADS // 2 - 2, (J, 4), (self.U, 2), (self.G, 2)):
            self.queries(False, False)
        self.queries(False, True)
        self.G.n = 0
        with repeat(a, HEADS // 2, (J, 34), (self.U, 4), (self.T, 50), (self.G, 2),
                    (self.B, 18), (self.O, 10), (self.F, 6)):
            self.head_pair()

    def queries(self, first, last):
        k = self.k
        for r in range(2):
            for h in range(2):
                if not first:
                    self.eng.wait_ge(k.q_spilled[2 * r + h], self.G.half() * 16)
                self.wide(k.tmp[:, 2 * r + h, :])
            self.split(double=(r == 1 and not last))
        self.G.step(2)

    def kv_hi(self, parts):
        k = self.k
        for dst, src in parts:
            r = self.act(dst, src)
        r.then_inc(k.kh_ready, 1)

    def keys_hi(self):
        k = self.k
        self.eng.wait_ge(k.mm_done, self.J.at(1))
        ps = k.sets[self.J.odd()]
        self.kv_hi([(k.kth[:, 0:480], ps[:, 0, 0:480]),
                    (k.kth[:, 480:].rearrange("p (b c) -> p b c", b=2), ps[:, 1:3, 0:464])])
        self.J.step()

    def queries_hi(self):
        k = self.k
        self.eng.wait_ge(k.q_loaded, self.G.at(1) * 16 * (BANKS + 1))
        for b in range(BANKS):
            self.act(k.qnh[:, b * CH:(b + 1) * CH], k.qld[b][:])
        self.act(k.qrp[:], k.qlr[:]).then_inc(k.qh_ready, 1)
        self.G.step()

    def head_pair(self):
        k, a, J = self.k, self.eng, self.J
        for h in range(2):
            if h == 0:
                self.queries_hi()
                self.keys_hi()
                for lo, n in ((0, 6), (6, 5)):
                    a.wait_ge(k.mm_done, J.at(1))
                    ps = k.sets[J.odd()]
                    self.kv_hi(v_parts(k.vh, ps, lo, n))
                    J.step()
            else:
                self.split()
                self.split()
            for s in range(-2, 9):
                job = s + 2 < 9
                if s >= 0:
                    self.turned(s, False)
                if job:
                    self.exponentials(s + 2)
                if s >= 2 and s % 2 == 0:
                    if job:
                        self.F.step()
                        a.wait_ge(k.of_ready, self.F.at())
                    else:
                        J.step()
                        a.wait_ge(k.freed[J.odd(-1)], J.half(-1) + 1)
                    self.out_hi(h, s // 2 - 1)
                if s >= 0:
                    self.turned(s, True)
                if s == 7 and h == 0:
                    self.keys_hi()
                    self.queries_hi()
                if job:
                    self.normalise(s + 2)
            J.step()
            a.wait_ge(k.freed[J.odd(-1)], J.half(-1) + 1)
            self.out_hi(h, None)
            self.B.step(9)
        J.step(4)
        self.split()
        J.step(4)
        self.split()

    def exponentials(self, s):
        k = self.k
        n = CTX if s == 8 else SMP + PAST
        self.eng.wait_ge(k.mm_done, self.J.at(1))
        ps = k.sets[self.J.odd()]
        self.eng.wait_ge(k.nb_ready, self.B.at(s + 1))
        src = ps[:, 0, 0:n] if s == 8 else ps[:].rearrange("p b c -> p (b c)")[:, 0:n]
        self.act(k.pr[s % 3][:, 0:n], src, ACT.Exp, bias=k.soft[:, 0, s % 2:s % 2 + 1], scale=SCALE,
                 accum_out=k.soft[:, 1, s % 2:s % 2 + 1]).then_inc(k.freed[self.J.odd()], 1)
        self.J.step()

    def normalise(self, s):
        k = self.k
        n = CTX if s == 8 else SMP + PAST
        self.eng.wait_ge(k.inv_ready, self.B.at(s + 1))
        self.act(k.pr[s % 3][:, 0:n], k.pr[s % 3][:, 0:n], scale=k.soft[:, 2, s % 2:s % 2 + 1]
                 ).then_inc(k.p_ready, 1)

    def turned(self, s, rest):
        k, T = self.k, self.T
        if s % 2 == 0 and s >= 2 and not rest:
            self.eng.wait_ge(k.mm_done, self.J.at(1))
        for g, end in prob_groups(s, rest):
            n = end - g
            self.eng.wait_ge(k.t_done, T.at(1))
            self.act(k.pth[:, g:g + n, s % 2, :],
                     k.tps[T.odd()][:, 0:n * P].rearrange("p (b c) -> p b c", b=n)
                     ).then_inc(k.pth_ready, 1)
            T.step()

    def out_hi(self, h, pair):
        k = self.k
        lo, n = (0, P) if pair is None else (P + 2 * P * pair, 2 * P)
        self.act(k.oh[:, h, lo:lo + n], k.of[self.O.odd()][:, 0:n]).then_inc(k.oh_ready, 1)
        self.O.step()


def prob_groups(s, rest):
    if s == 8:
        return [] if rest else [(0, 1)]
    return [(8, 10)] if rest else [(0, 4), (4, 8)]


def v_parts(dst, ps, lo, n):
    out = []
    for b in range(0, n, 2):
        m = min(2, n - b)
        out.append((dst[:, lo + b:lo + b + m, :, :].rearrange("p b h c -> p (b h c)"),
                    ps[:, b // 2, 0:m * 256]))
    return out


class Elementwise(Engine):
    def then(self, ins):
        ins.then_inc(self.k.dv_step, 1)
        self.L.step()
        self.eng.wait_ge(self.k.dv_step, self.L.at())

    def free(self, last):
        last.then_inc(self.k.freed[self.J.odd()], 1)
        self.J.step()

    def split(self, double=False):
        k, s = self.k, self.U.odd()
        self.U.step()
        self.eng.wait_ge(k.hi_done, self.U.at())
        if double:
            o, h = (w[:, s, :].rearrange("p (k a c) -> p k a c", a=2, c=ROPE) for w in (k.wlo, k.whi))
            i = k.wraw[:, s, 0:512].rearrange("p (k a c) -> p k a c", a=1, c=ROPE
                                              ).to_broadcast([P, DT, 2, ROPE])
        else:
            o, h, i = k.wlo[:, s, :], k.whi[:, s, :], k.wraw[:, s, :]
        self.nc.vector.tensor_tensor(o, i, h, ALU.subtract).then_inc(k.lo_done, 1)

    def sum_squares(self, first):
        k, v = self.k, self.nc.vector
        sq = k.tmp[:, 2 + self.Q.odd(), :]
        self.S.step()
        self.eng.wait_ge(k.sq_ready, self.S.at())
        r = v.tensor_copy(k.acc[:], sq) if first else v.tensor_tensor(k.acc[:], k.acc[:], sq, ALU.add)
        r.then_inc(k.sq_used, 1)
        self.Q.step()
        self.eng.wait_ge(k.sq_used, self.Q.at())

    def mean(self, out, src, width):
        k = self.k
        s, n = self.J.odd(), self.J.half() + 1
        self.free(self.nc.vector.tensor_scalar(out, src, 1.0 / width, EPS, ALU.mult, ALU.add))
        self.eng.wait_ge(k.freed[s], n)
        self.nc.vector.reciprocal(out, out).then_inc(k.rs_ready, 1)
        self.R.step()
        self.eng.wait_ge(k.rt_ready, self.R.n)

    def mean_rstd(self, width):
        k, v = self.k, self.nc.vector
        self.eng.wait_ge(k.mm_done, self.J.at(1))
        self.mean(k.rv[:], k.sets[self.J.odd()][:, 0, 0:NB], width)
        v.tensor_tensor(k.acc[:].rearrange("p (b c) -> p b c", c=P),
                        k.ident[:].unsqueeze(1).to_broadcast([P, NB, P]),
                        k.rv[:].unsqueeze(2).to_broadcast([P, NB, P]), ALU.mult).then_inc(k.diag_ready, 1)
        self.eng.wait_ge(k.mm_done, self.J.at(1))
        self.free(v.tensor_copy(k.rstd[:].rearrange("p (b c) -> p b c", b=BANKS),
                                k.sets[self.J.odd()][:, :, 0:CH]))
        self.eng.wait_ge(k.freed[self.J.odd(-1)], self.J.half(-1) + 1)

    def norm(self, layer, gains, scale, squared=False, rooted=False):
        k, dve, v = self.k, self.eng, self.nc.vector
        s = layer * ADA + scale
        g = gains + layer * DT
        v.scalar_tensor_tensor(k.gain[:], k.mod[:, s:s + DT, :], 1.0,
                               k.vecs[:, g:g + DT].unsqueeze(2).to_broadcast([P, DT, 2]),
                               ALU.add, ALU.mult)
        if not rooted:
            for n in range(DT - 1 if squared else 0, DT):
                self.sum_squares(n == 0)
            self.mean_rstd(D)
        for n in range(DT + 1):
            if n < DT:
                if n >= 2:
                    dve.wait_ge(k.hf_ready, 2 * (self.E.n + n - 1))
                v.tensor_tensor(k.tmp[:, n % 2, :], k.x[:, n, :], k.rstd[:], ALU.mult
                                ).then_inc(k.n_ready, 1)
            if n >= 1:
                dve.wait_ge(k.hh_ready, self.H.n + n)
                v.tensor_tensor(k.hlo[:, n - 1, :], k.tmp[:, 2 + (n - 1) % 2, :], k.hhi[:, n - 1, :],
                                ALU.subtract).then_inc(k.h_ready, 1)
        self.H.step(DT)
        self.E.step(DT)

    def program(self):
        k, dve, v, T = self.k, self.eng, self.nc.vector, self.T
        v.memset(k.ones[:], 1.0).then_inc(k.ones_set, 1)
        dve.wait_ge(k.t_free[0], 1)
        for n in range(2):
            dve.wait_ge(k.t_done, 3 + n)
            v.tensor_copy(k.wst[:, 4 * n:4 * n + 4, :],
                          k.tps[n][:].rearrange("p (g c) -> p g c", g=4)).then_inc(k.t_free[n], 1)
        for n in range(NB):
            dve.wait_ge(k.t_done, 4 + 2 * n + 2)
            v.tensor_copy(k.x[:, 4:8, n * P:(n + 1) * P], k.tps[1][:].rearrange("p (f c) -> p f c", f=4)
                          ).then_inc(k.t_free[1], 1)
        T.step(4 + 2 * NB)
        for n in range(DT):
            self.sum_squares(n == 0)
        self.mean_rstd(D)
        for n in range(1, ADA_HEAD // 2, 2):
            dve.wait_ge(k.al_loaded[n % 4], 16 * (n // 4 + 1))
            w = k.aldr[:, n % 4, :].rearrange("p (k u c) -> p k u c", k=DT, c=P)
            for i in range(DT):
                for c in range(2):
                    out, x = k.pah[:, n // 2, :, c, :], k.cond[:, i, c:c + 1]
                    if i == 0:
                        r = v.tensor_scalar(out, w[:, i], x, None, ALU.mult)
                    else:
                        dve.wait_ge(k.dv_step, self.L.at(0 if i == DT - 1 and c == 1 else -1))
                        r = v.scalar_tensor_tensor(out, w[:, i], x, out, ALU.mult, ALU.add)
                    if i < DT - 1:
                        r.then_inc(k.dv_step, 1)
                        self.L.step()
            r.then_inc(k.al_summed, 1)
        self.split()
        self.split()
        dve.wait_ge(k.al_used, ADA_HEAD // 2)
        v.tensor_tensor(k.mod[:, 0:ADA_HEAD, :],
                        k.sets[0][:, 0, 0:2 * ADA_HEAD].rearrange("p (t c) -> p t c", c=2),
                        k.bias[:, 0:ADA_HEAD].unsqueeze(2).to_broadcast([P, ADA_HEAD, 2]), ALU.add
                        ).then_inc(k.al_read, 1)
        dve.wait_ge(k.al_read, 1)
        self.mixer()
        self.ffn(0)
        self.attention()
        self.ffn(1)
        self.sum_squares(False)
        self.mean_rstd(D)
        for n in range(DT + 1):
            if n < DT:
                v.scalar_tensor_tensor(k.tmp[:, n % 4, :], k.x[:, n, :], k.vecs[:, V_FG + n:V_FG + n + 1],
                                       k.rstd[:], ALU.mult, ALU.mult).then_inc(k.y_ready, 1)
            if n >= 1:
                m = n - 1
                if m >= 2:
                    dve.wait_ge(k.y_stored[m % 2], 32 * (m // 2))
                for g in range(3):
                    dve.wait_ge(k.t_done, T.n + 1)
                    v.tensor_copy(k.yst[:, m % 2, 3 * g:3 * g + 3, :].rearrange("p b c -> p (b c)"),
                                  k.tps[T.odd()][:, 0:CH]).then_inc(k.t_free[T.odd()], 1)
                    T.step()

    def ada(self, tile, n):
        k = self.k
        self.eng.wait_ge(k.mm_done, self.J.at(1))
        ps = k.sets[self.J.odd()]
        self.free(self.nc.vector.tensor_tensor(
            k.mod[:, bass.ds(tile, n), :], ps[:, 0, 0:2 * n].rearrange("p (t c) -> p t c", c=2),
            k.bias[:, bass.ds(tile, n)].unsqueeze(2).to_broadcast([P, n, 2]), ALU.add))

    def ada_sums(self, raw, n):
        k, dve, v, slot = self.k, self.eng, self.nc.vector, self.V.odd()
        dve.wait_ge(k.ad_loaded[slot], self.loaded[slot].at(n) * 16)
        self.loaded[slot].step(n)
        for i in range(DT):
            for c in range(2):
                out, w = k.pa[:, slot, 0:n, c, :], raw[:, :, i * P:(i + 1) * P]
                x = k.cond[:, i, c:c + 1]
                if i == 0:
                    r = v.tensor_scalar(out, w, x, None, ALU.mult)
                else:
                    dve.wait_ge(k.dv_step, self.L.at(0 if i == DT - 1 and c == 1 else -1))
                    r = v.scalar_tensor_tensor(out, w, x, out, ALU.mult, ALU.add)
                if i < DT - 1:
                    r.then_inc(k.dv_step, 1)
                    self.L.step()
        r.then_inc(k.ad_summed, 1)
        self.V.step()

    def out_tiles(self, gate, half, final=False):
        k, v = self.k, self.nc.vector
        for n in range(half * 4, half * 4 + 4):
            self.eng.wait_ge(k.mm_done, self.J.at(1))
            ps = k.sets[self.J.odd()]
            for lo, hi, c in PARTS:
                src = span(ps, lo, hi)
                dst = k.x[:, n, lo:hi]
                if hi - lo > CH:
                    dst = dst.rearrange("p (b c) -> p b c", c=CH)
                last = v.scalar_tensor_tensor(dst, src, k.mod[:, gate + n, c:c + 1], dst,
                                              ALU.mult, ALU.add)
            self.free(last)
            if final and n >= 1:
                self.sum_squares(n == 1)

    def scale_v(self, m, times):
        k = self.k
        self.eng.wait_ge(k.v_loaded[m], times)
        vt = k.vld[:, m, :].rearrange("p (b c) -> p b c", b=NB)
        self.nc.vector.tensor_tensor(vt, vt, k.rv[:].unsqueeze(2).to_broadcast([P, NB, P]), ALU.mult
                                     ).then_inc(k.vs_ready, 1)

    def hidden_lo(self, h):
        k = self.k
        self.A.step()
        self.eng.wait_ge(k.ah_ready, self.A.at())
        self.nc.vector.tensor_tensor(k.glo[:, h, :], k.tmp[:, 1, :], k.ghi[:, h, :], ALU.subtract
                                     ).then_inc(k.a_ready, 1)

    def mixer(self):
        k, dve, v, J, T = self.k, self.eng, self.nc.vector, self.J, self.T
        self.norm(0, V_N1, SC1, rooted=True)
        self.then(v.memset(k.acc[:], 0.0))
        self.v_turn(0, True)
        with repeat(dve, GT // 2 - 1, (J, 4), (self.U, 2), (self.Q, 2), (self.S, 2), (T, 6),
                    (self.V, 2), (self.L, 28), (self.loaded[0], 2), (self.loaded[1], 2)) as i:
            self.v_turn(i + 1, False)
        self.eng.wait_ge(k.mm_done, self.J.at(1))
        ps = k.sets[self.J.odd()]
        self.mean(k.rv[:], ps[:, 0, 0:NB], AW)
        self.scale_v(0, 16)
        self.ada_sums(k.adu, 2)
        J.step()
        self.split()
        with repeat(dve, GT // 2 - 1, (J, 16), (self.U, 4), (self.A, 2), (self.L, 2 + 56),
                    (self.V, 4), (self.loaded[0], 4), (self.loaded[1], 2)) as i:
            self.mixer_turn(i, False)
        self.mixer_turn(GT // 2 - 1, True)

    def v_turn(self, turn, first):
        k, dve, v, J, T = self.k, self.eng, self.nc.vector, self.J, self.T
        for h in range(2):
            self.ada_sums((k.adv, k.adu)[h], 2)
            J.step()
            self.ada(ADA_HEAD + 4 * turn + 2 * h, 2)
            if not first:
                dve.wait_ge(k.spilled[h], 16 * turn)
            for g in range(3):
                dve.wait_ge(k.t_done, T.at(1))
                v.tensor_copy(k.vst[:, h, g * CH:(g + 1) * CH], k.tps[T.odd()][:, 0:CH]
                              ).then_inc(k.t_free[T.odd()], 1)
                T.step()
            self.sum_squares(False)
            self.split()

    def mixed(self, i, m, last, *ada):
        k, v = self.k, self.nc.vector
        self.J.step()
        for tile, n in ada:
            self.ada(tile, n)
        job = -1 - len(ada)
        self.eng.wait_ge(k.freed[self.J.odd(job)], self.J.half(job) + 1)
        s = k.tmp[:, 2, :].rearrange("p (b c) -> p b c", b=NB)
        self.then(v.tensor_tensor(s, s, k.bsb[:, i, :].unsqueeze(1).to_broadcast([P, NB, P]), ALU.add))
        v.tensor_tensor(k.tmp[:, 1, :], k.tmp[:, 2, :], k.tmp[:, 0, :], ALU.mult).then_inc(k.af_ready, 1)
        if not last:
            self.scale_v(1 - m, 16 * (i + 1 + m))
        self.hidden_lo(m)

    def mixer_turn(self, i, last):
        k, J = self.k, self.J
        self.mixed(i, 0, False, (ADA + 6 * i, 2))
        self.ada_sums(self.k.tmp[:, 3:4, 0:UNIT], 1)
        self.ada_sums(self.k.adu, 2)
        J.step()
        self.split()
        self.mixed(i, 1, last, (ADA + 6 * i + 2, 1), (ADA + 6 * i + 3, 2))
        self.ada_sums(self.k.tmp[:, 3:4, 0:UNIT], 1)
        if not last:
            self.ada_sums(self.k.adu, 2)
            J.step()
            self.split()
        self.ada(ADA + 6 * i + 5, 1)
        self.out_tiles(G1, 0, last)
        self.split()
        self.out_tiles(G1, 1, last)
        self.split()

    def up(self, h):
        k = self.k
        self.eng.wait_ge(k.mm_done, self.J.at(1))
        ps = k.sets[self.J.odd()]
        self.eng.wait_ge(k.freed[self.J.odd(-1)], self.J.half(-1) + 1)
        self.free(self.nc.vector.tensor_tensor(
            k.tmp[:, 1, :].rearrange("p (b c) -> p b c", b=BANKS), ps[:, :, 0:CH],
            k.tmp[:, 0, :].rearrange("p (b c) -> p b c", b=BANKS), ALU.mult))
        self.hidden_lo(h)

    def ffn_turn(self, gate, last, doubled=None):
        J = self.J
        self.up(0)
        self.split()
        J.step()
        self.split()
        self.up(1)
        self.split()
        if not last:
            J.step()
            self.split()
        self.out_tiles(gate, 0, last)
        if not last or doubled is not None:
            self.split(double=bool(doubled))
        self.out_tiles(gate, 1, last)
        if not last or doubled is not None:
            self.split()

    def ffn(self, layer):
        self.norm(layer, V_N2, SC2, layer == 0)
        self.J.step()
        self.split()
        gate = layer * ADA + G2
        with repeat(self.eng, FT // 2 - 1, (self.J, 12), (self.U, 6), (self.A, 2)):
            self.ffn_turn(gate, False)
        self.ffn_turn(gate, True, doubled=True if layer == 0 else None)

    def rotate(self, out, t, by_cos, partner, cos, sin):
        v = self.nc.vector
        v.tensor_tensor(by_cos, t, cos, ALU.mult)
        self.then(v.stream_shuffle(partner, t, SWAP))
        self.then(v.tensor_tensor(partner, partner, sin, ALU.mult))
        return v.tensor_tensor(out, by_cos, partner, ALU.add)

    def square_into_acc(self, src, first):
        k, v = self.k, self.nc.vector
        if first:
            v.tensor_tensor(k.acc[:], src, src, ALU.mult).then_inc(k.sq_used, 1)
        else:
            self.then(v.tensor_tensor(k.rstd[:], src, src, ALU.mult))
            v.tensor_tensor(k.acc[:], k.acc[:], k.rstd[:], ALU.add).then_inc(k.sq_used, 1)
        self.Q.step()
        self.eng.wait_ge(k.sq_used, self.Q.at())

    def attention(self):
        k, dve, v, J, T = self.k, self.eng, self.nc.vector, self.J, self.T
        self.norm(1, V_N1, SC1, True)
        J.step()
        self.eng.wait_ge(k.freed[self.J.odd(-1)], self.J.half(-1) + 1)
        dve.wait_ge(k.rope_loaded, 16)
        self.split()
        t0, t2 = k.tmp[:, 0, :], k.tmp[:, 2, :]
        self.rotate(t2, t0, t2, k.tmp[:, 1, :], k.csk[:, 0, :], k.csk[:, 1, :]).then_inc(k.ck_ready, 1)
        dve.wait_ge(k.ck_ready, 1)
        dve.wait_ge(k.kh_ready, 1)
        v.tensor_tensor(k.krl[:, 0:TOK], t2, k.krh[:, 0:TOK], ALU.subtract)
        for m in range(CT):
            J.step()
            self.split()
            self.eng.wait_ge(k.freed[self.J.odd(-1)], self.J.half(-1) + 1)
            self.square_into_acc(k.ckf[:, m, :], m == 0)
        dve.wait_ge(k.kh_ready, 2)
        v.tensor_tensor(k.ckl[:, :, TOK:], k.tps[T.odd()][:, 0:CT * PAST].rearrange("p (m c) -> p m c", m=CT),
                        k.ckh[:, :, TOK:], ALU.subtract).then_inc(k.t_free[T.odd()], 1)
        T.step()
        dve.wait_ge(k.kh_ready, 3)
        v.tensor_tensor(k.krl[:, TOK:], k.tps[T.odd()][:, 0:PAST], k.krh[:, TOK:], ALU.subtract
                        ).then_inc(k.t_free[T.odd()], 1)
        T.step()
        dve.wait_ge(k.t_done, T.at(1))
        v.tensor_copy(k.nck[:, KVL:], k.tps[T.odd()][:, 0:ROPE]).then_inc(k.t_free[T.odd()], 1)
        T.step()
        J.step()
        self.split()
        self.mean_rstd(KVL)
        for m in range(CT):
            v.scalar_tensor_tensor(k.ckf[:, m, :], k.ckf[:, m, :], k.vecs[:, V_KVG + m:V_KVG + m + 1],
                                   k.rstd[:], ALU.mult, ALU.mult).then_inc(k.ck_ready, 1)
        for m in range(CT):
            dve.wait_ge(k.kh_ready, 4 + m)
            v.tensor_tensor(k.ckl[:, m, 0:TOK], k.ckf[:, m, :], k.ckh[:, m, 0:TOK], ALU.subtract)
        self.square_into_acc(k.tmp[:, 0, :], True)
        for m in range(1, QT):
            J.step()
            self.eng.wait_ge(k.freed[self.J.odd(-1)], self.J.half(-1) + 1)
            self.square_into_acc(k.tmp[:, m, :], False)
            self.split(double=m == QT - 1)
        dve.wait_ge(k.t_done, T.at(1))
        v.tensor_copy(k.nck[:, 0:KVL], k.tps[T.odd()][:, 0:KVL]).then_inc(k.t_free[T.odd()], 1)
        T.step()
        self.mean_rstd(QL)
        for m in range(QT):
            v.scalar_tensor_tensor(k.tmp[:, m, :], k.tmp[:, m, :], k.vecs[:, V_QG + m:V_QG + m + 1],
                                   k.rstd[:], ALU.mult, ALU.mult).then_inc(k.n_ready, 1)
        for m in range(QT):
            dve.wait_ge(k.hh_ready, self.H.n + m + 1)
            v.tensor_tensor(k.qal[:, m, :], k.tmp[:, m, :], k.qah[:, m, :], ALU.subtract
                            ).then_inc(k.h_ready, 1)
        self.H.step(QT)
        dve.wait_ge(k.rope_loaded, 32)
        self.queries(True, False)
        with repeat(dve, HEADS // 2 - 2, (J, 4), (self.U, 2), (self.L, 4), (self.W, 2)):
            self.queries(False, False)
        self.queries(False, True)
        with repeat(dve, HEADS // 2, (J, 34), (self.U, 4), (T, 50), (self.G, 2), (self.B, 18),
                    (self.O, 10), (self.F, 6), (self.L, 18), (self.K, 4)):
            self.head_pair()

    def queries(self, first, last):
        k, J = self.k, self.J
        J.step(2)
        self.split()
        for h in range(2):
            J.step()
            self.eng.wait_ge(k.freed[self.J.odd(-1)], self.J.half(-1) + 1)
            if not first or h:
                self.eng.wait_ge(k.qf_ready, self.W.at())
            self.W.step()
            t = k.tmp[:, 2 + h, :]
            self.rotate(t, t, k.rstd[:], k.acc[:], k.cs[:, 0, :], k.cs[:, 1, :]).then_inc(k.qf_ready, 1)
        self.split(double=not last)

    def kv_lo(self, parts):
        k = self.k
        self.K.step()
        self.eng.wait_ge(k.kh_ready, self.K.at(5))
        for dst, hi, src in parts:
            last = self.nc.vector.tensor_tensor(dst, src, hi, ALU.subtract)
        self.free(last)

    def keys_lo(self):
        k = self.k
        self.eng.wait_ge(k.mm_done, self.J.at(1))
        ps = k.sets[self.J.odd()]
        self.kv_lo([(k.ktl[:, 0:480], k.kth[:, 0:480], ps[:, 0, 0:480]),
                    (k.ktl[:, 480:].rearrange("p (b c) -> p b c", b=2),
                     k.kth[:, 480:].rearrange("p (b c) -> p b c", b=2), ps[:, 1:3, 0:464])])

    def queries_lo(self):
        k, v = self.k, self.nc.vector
        self.G.step()
        self.eng.wait_ge(k.qh_ready, self.G.at())
        for b in range(BANKS):
            c = slice(b * CH, (b + 1) * CH)
            v.tensor_tensor(k.qnl[:, c], k.qld[b][:], k.qnh[:, c], ALU.subtract)
        v.tensor_tensor(k.qrp[ROPE:P, :], k.qlr[ROPE:P, :], k.qrp[ROPE:P, :], ALU.subtract
                        ).then_inc(k.q_ready, 1)

    def head_pair(self):
        k, dve, v, J = self.k, self.eng, self.nc.vector, self.J
        for h in range(2):
            if h == 0:
                self.keys_lo()
                self.queries_lo()
                for lo, n in ((0, 6), (6, 5)):
                    dve.wait_ge(k.mm_done, J.at(1))
                    ps = k.sets[J.odd()]
                    self.kv_lo([(a, b, c) for (a, c), (b, _) in
                                zip(v_parts(k.vl, ps, lo, n), v_parts(k.vh, ps, lo, n))])
            else:
                self.split()
                self.split()
            for s in range(-2, 9):
                job, out = s + 2 < 9, s >= 2 and s % 2 == 0
                if job:
                    self.maxima(s + 2, out)
                elif out:
                    dve.wait_ge(k.mm_done, J.at(1))
                    ps = k.sets[J.odd()]
                    self.free(v.tensor_copy(k.of[self.O.odd()][:], ps[:, 2, 256:512]))
                if s >= 0:
                    self.turned(s, False)
                if job:
                    self.inverse_sum(s + 2)
                if out:
                    self.out_lo(h, s // 2 - 1)
                if s >= 0:
                    self.turned(s, True)
                if s == 7 and h == 0:
                    self.keys_lo()
                    self.queries_lo()
            dve.wait_ge(k.mm_done, J.at(1))
            ps = k.sets[J.odd()]
            self.free(v.tensor_copy(k.of[self.O.odd()][:, 0:P], ps[:, 2, 256:256 + P]))
            self.out_lo(h, None)
            self.B.step(9)
        self.out_tiles(ADA + G1, 0)
        self.split()
        self.out_tiles(ADA + G1, 1)
        self.split()

    def maxima(self, s, out):
        k, v = self.k, self.nc.vector
        n = CTX if s == 8 else SMP + PAST
        self.eng.wait_ge(k.mm_done, self.J.at(1))
        ps = k.sets[self.J.odd()]
        src = ps[:, 0, 0:n] if s == 8 else ps[:].rearrange("p b c -> p (b c)")[:, 0:n]
        nmax = k.soft[:, 3, s % 2:s % 2 + 1]
        if out:
            v.tensor_copy(k.of[self.O.odd()][:], ps[:, 2, 256:512]).then_inc(k.of_ready, 1)
            self.F.step()
        self.then(v.reduce_max(nmax, src, AX_X, negate=True))
        v.tensor_scalar(k.soft[:, 0, s % 2:s % 2 + 1], nmax, SCALE, None, ALU.mult).then_inc(k.nb_ready, 1)
        self.J.step()

    def inverse_sum(self, s):
        k = self.k
        self.eng.wait_ge(k.freed[self.J.odd(-1)], self.J.half(-1) + 1)
        self.nc.vector.reciprocal(k.soft[:, 2, s % 2:s % 2 + 1], k.soft[:, 1, s % 2:s % 2 + 1]
                                  ).then_inc(k.inv_ready, 1)

    def turned(self, s, rest):
        k, T = self.k, self.T
        for g, end in prob_groups(s, rest):
            n = end - g
            self.eng.wait_ge(k.pth_ready, T.at(1 - T0_PROBS))
            self.nc.vector.tensor_tensor(k.ptl[:, g:g + n, s % 2, :],
                                         k.tps[T.odd()][:, 0:n * P].rearrange("p (b c) -> p b c", b=n),
                                         k.pth[:, g:g + n, s % 2, :], ALU.subtract
                                         ).then_inc(k.t_free[T.odd()], 1)
            T.step()

    def out_lo(self, h, pair):
        k = self.k
        lo, n = (0, P) if pair is None else (P + 2 * P * pair, 2 * P)
        o = self.O.odd()
        self.O.step()
        self.eng.wait_ge(k.oh_ready, self.O.at())
        self.nc.vector.tensor_tensor(k.ol[:, h, lo:lo + n], k.of[o][:, 0:n], k.oh[:, h, lo:lo + n],
                                     ALU.subtract).then_inc(k.o_ready, 1)


class Moves(Engine):

    def program(self):
        k, g, J, T, d = self.k, self.eng, self.J, self.T, self.k.d
        T.step(4 + 2 * NB)
        J.step(2)
        with repeat(g, GT // 2, (J, 4), (T, 6)) as i:
            for h in range(2):
                T.step(3)
                g.wait_ge(k.t_free[T.odd(-1)], T.half(-1) + 1)
                g.wait_ge(k.t_free[T.odd(-2)], T.half(-2) + 1)
                g.dma_start(k.v_dram[2 * i + h], k.vst[:, h, :]).then_inc(k.spilled[h], 16)
                J.step(2)
        J.step(2)
        for h in range(2):
            g.wait_ge(k.spilled[h], 16 * (GT // 2))
        for h in range(2):
            g.dma_start(k.vld[:, h, :], k.v_dram[h]).then_inc(k.v_loaded[h], 16)
        with repeat(g, GT // 2 - 1, (J, 16)) as i:
            for h in range(2):
                g.wait_ge(k.mm_done, J.at(1 + 3 * h))
                g.dma_start(k.vld[:, h, :], k.v_dram[2 * i + 2 + h]).then_inc(k.v_loaded[h], 16)
            J.step(16)
        J.step(15)
        J.step(3 + 12 * (FT // 2 - 1) + 11 + 2)
        g.wait_ge(k.h_ready, 3 * DT)
        g.dma_start(k.csk[:], d["rope"].rearrange("a p n -> p a n")).then_inc(k.rope_loaded, 16)
        g.dma_start(k.cin[:], d["cache_ckv"][0, 0].rearrange("(b p) n -> p b n", p=P)
                    ).then_inc(k.cache_loaded, 16)
        for c in range(2):
            g.dma_start(k.kin[:, :, c * ROPE:(c + 1) * ROPE],
                        d["cache_krope"][0, 0].rearrange("(b p) n -> p b n", p=P)
                        ).then_inc(k.cache_loaded, 16)
        g.wait_ge(k.t_free[T.odd(2)], T.half(2) + 1)
        g.dma_start(d["new_krope"][0, 0], k.nck[:, KVL:]).then_inc(k.stored, 16)
        g.wait_ge(k.t_free[T.odd(3)], T.half(3) + 1)
        g.dma_start(d["new_ckv"][0, 0], k.nck[:, 0:KVL]).then_inc(k.stored, 16)
        T.step(4)
        J.step(1 + CT + 1 + 2 + QT - 1 + 2)
        g.wait_ge(k.mm_done, J.at())
        g.dma_start(k.cs[:], d["rope"].rearrange("a p n -> p a n")).then_inc(k.rope_loaded, 16)
        with repeat(g, HEADS // 2, (J, 4), (self.G, 2)) as i:
            for h in range(2):
                J.step()
                self.eng.wait_ge(k.freed[self.J.odd(-1)], self.J.half(-1) + 1)
                g.dma_start(k.q_dram[2 * i + h, 0], k.tmp[:, h, :]).then_inc(k.q_spilled[h], 16)
            for h in range(2):
                J.step()
                self.G.step()
                g.wait_ge(k.qf_ready, self.G.at())
                g.dma_start(k.q_dram[2 * i + h, 1], k.tmp[:, 2 + h, :]).then_inc(k.q_spilled[2 + h], 16)
        self.G.n = 0
        for n in range(4):
            g.wait_ge(k.q_spilled[n], 16 * (HEADS // 2))
        for b in range(BANKS):
            g.dma_start(k.qld[b][:], k.q_dram[0, 0, :, b * CH:(b + 1) * CH]).then_inc(k.q_loaded, 16)
        g.dma_start(k.qlr[:], k.q_dram[0, 1]).then_inc(k.q_loaded, 16)
        with repeat(g, HEADS - 1) as i:
            g.wait_ge(k.q_ready, i + 1)
            for b in range(BANKS):
                g.dma_start(k.qld[b][:], k.q_dram[i + 1, 0, :, b * CH:(b + 1) * CH]
                            ).then_inc(k.q_loaded, 16)
            g.dma_start(k.qlr[:], k.q_dram[i + 1, 1]).then_inc(k.q_loaded, 16)
        J.step(34 * (HEADS // 2) + 3 + 12 * (FT // 2 - 1) + 11 + 2)
        T.step(50 * (HEADS // 2))
        for n in range(DT):
            T.step(3)
            g.wait_ge(k.t_free[T.odd(-1)], T.half(-1) + 1)
            g.wait_ge(k.t_free[T.odd(-2)], T.half(-2) + 1)
            c = slice(n * P, (n + 1) * P)
            g.dma_start(d["y_prompt"][0, :, c], k.yst[:, n % 2, 0, :]).then_inc(k.y_stored[n % 2], 16)
            g.dma_start(d["y_sample"][0, :, c].rearrange("(b p) n -> p b n", p=P), k.yst[:, n % 2, 1:NB, :]
                        ).then_inc(k.y_stored[n % 2], 16)
        g.wait_ge(k.stored, 32)
        for n in range(2):
            g.wait_ge(k.y_stored[n], 32 * DT // 2)


def two_layers(nc, d):
    with ExitStack() as stack:
        k = Kernel(nc, d, stack)
        block = stack.enter_context(nc.Block())

        @block.sync
        def _(eng):
            Loads(k, eng).program()

        @block.tensor
        def _(eng):
            Products(k, eng).program()

        @block.scalar
        def _(eng):
            Activations(k, eng).program()

        @block.vector
        def _(eng):
            Elementwise(k, eng).program()

        @block.gpsimd
        def _(eng):
            Moves(k, eng).program()


def rope_tables():
    pairs, grid = ROPE // 4, 64
    inv = (1.0 / (np.float32(10000.0) ** (np.arange(pairs, dtype=np.float32) / np.float32(pairs)))
           ).astype(np.float32)
    n = np.arange(SMP)
    pos = np.stack([n // grid, n % grid]).astype(np.float32)
    out = np.zeros((2, P, TOK), np.float32)
    out[0] = 1.0
    for p in range(P):
        axis, half, i = p % ROPE // 32, p % 32 // 16, p % 16
        angle = (pos[axis] * inv[i]).astype(np.float32).astype(np.float64)
        out[0, p, CTX:] = np.cos(angle)
        out[1, p, CTX:] = np.sin(angle) * (1 if half else -1)
    return out


_INS = ["x_prompt", "x_sample", "cache_ckv", "cache_krope", "c", "c_ctx", "ada_w", "ada_b", "norm1_g",
        "norm2_g", "a_w_in", "a_v_g", "a_w_s", "a_b_s", "a_w_out", "b_w_dq", "b_q_g", "b_w_uq",
        "b_w_dkv", "b_kv_g", "b_w_ukv", "b_w_o", "f_w_in", "f_w_out", "final_g"]
_OUTS = [("y_prompt", (1, CTX, D)), ("y_sample", (1, SMP, D)), ("new_ckv", (1, 1, CTX, KVL)),
         ("new_krope", (1, 1, CTX, ROPE))]


def kernel(**inputs):
    import concourse.bacc as _bacc
    from concourse.bass_utils import run_bass_kernel_spmd as _run

    nc = _bacc.Bacc("TRN2", target_bir_lowering=False, num_devices=1)
    arrays = {f"in_{n}": np.ascontiguousarray(inputs[n]) for n in _INS}
    arrays["in_rope"] = rope_tables()
    arrays["in_ident"] = np.eye(P, dtype=np.float32)
    d = {n[3:]: nc.dram_tensor(n, a.shape, F32, kind="ExternalInput").ap() for n, a in arrays.items()}
    for name, shape in _OUTS:
        d[name] = nc.dram_tensor(name, shape, F32, kind="ExternalOutput").ap()
    two_layers(nc, d)
    r = _run(nc, [arrays], core_ids=[0])
    return tuple(r.results[0][name] for name, _ in _OUTS)
```
